# Optimizing a Trainium2 kernel written in Bass

```python
import math
import jax, jax.numpy as jnp
from jax import lax
import numpy as np

D_MODEL = 1024
BATCH = 1
SEQ = 256
DEPTH = 2

HEAD_DIM = 64
A_HEADS = D_MODEL // (2 * HEAD_DIM)
DILATED_BRANCHES = ((128, 1), (512, 4), (2048, 16))
DIFF_HALF = 64
DIFF_VDIM = 2 * DIFF_HALF
B_HEADS = D_MODEL // (2 * DIFF_VDIM)
C_HEADS = D_MODEL // HEAD_DIM
Q_BLOCK = 128
N_BUCKETS = 32
MAX_DISTANCE = 2048
BIAS_HEADS = A_HEADS + B_HEADS
PEER_HEADS = 8
N_KEYS = 128
N_EXPERTS = N_KEYS * N_KEYS
PEER_TOPK = 16
PEER_KEY_HALF = 128
PEER_CHUNK = 128
RMS_EPS = 1e-6
NEG_INF = -1e30
FORGET_BIAS_INIT = 3.0
A_WIDTH = A_HEADS * HEAD_DIM
B_QK_WIDTH = B_HEADS * 2 * DIFF_HALF
B_V_WIDTH = B_HEADS * DIFF_VDIM
EVEN_IN = 3 * A_WIDTH + 2 * B_QK_WIDTH + B_V_WIDTH
EVEN_MIX = A_WIDTH + B_V_WIDTH
C_WIDTH = C_HEADS * HEAD_DIM
ODD_IN = 3 * C_WIDTH + C_HEADS

kernel_name = 'hybrid_dilated_diff_fox_peer'

def rms_norm(x, g):
    x32 = x.astype(jnp.float32)
    y = x32 * lax.rsqrt(jnp.mean(x32 * x32, axis=-1, keepdims=True) + RMS_EPS)
    return (y * g.astype(jnp.float32)).astype(x.dtype)

def t5_bucket(dist):
    max_exact = N_BUCKETS // 2
    d = jnp.maximum(dist, 1).astype(jnp.float32)
    large = max_exact + (jnp.log(d / max_exact) / math.log(MAX_DISTANCE / max_exact)
                         * (N_BUCKETS - max_exact)).astype(jnp.int32)
    large = jnp.minimum(large, N_BUCKETS - 1)
    return jnp.where(dist < max_exact, dist, large)

def split_heads(t, n_heads):
    b, s, _ = t.shape
    return t.reshape(b, s, n_heads, -1).transpose(0, 2, 1, 3)

def sweep_query_blocks(fn, q):
    b, h, s, dq = q.shape
    nb = s // Q_BLOCK
    qb = q.reshape(b, h, nb, Q_BLOCK, dq).transpose(2, 0, 1, 3, 4)
    out = lax.map(lambda a: fn(a[0], a[1]), (jnp.arange(nb, dtype=jnp.int32), qb))
    out = out.transpose(1, 0, 3, 2, 4)
    return out.reshape(b, s, h * out.shape[-1])

def dilated_attention(q, k, v, bias_table):
    scale = HEAD_DIM ** -0.5
    branch_offs = [d * jnp.arange(w // d + 1, dtype=jnp.int32) for (w, d) in DILATED_BRANCHES]
    branch_bias = [bias_table[t5_bucket(o)].T for o in branch_offs]

    def block(bi, qblk):
        pos = bi * Q_BLOCK + jnp.arange(Q_BLOCK, dtype=jnp.int32)
        outs, lses = [], []
        for offs, bb in zip(branch_offs, branch_bias):
            idx = pos[:, None] - offs[None, :]
            valid = idx >= 0
            idx = jnp.maximum(idx, 0)
            kg = k[:, :, idx]
            vg = v[:, :, idx]
            logits = jnp.einsum('bhqd,bhqnd->bhqn', qblk, kg).astype(jnp.float32) * scale
            logits = jnp.where(valid, logits + bb[None, :, None, :].astype(jnp.float32), NEG_INF)
            lse = jax.nn.logsumexp(logits, axis=-1, keepdims=True)
            p = jnp.exp(logits - lse)
            outs.append(jnp.einsum('bhqn,bhqnd->bhqd', p.astype(v.dtype), vg).astype(jnp.float32))
            lses.append(lse)
        wts = jax.nn.softmax(jnp.stack(lses), axis=0)
        return jnp.sum(wts * jnp.stack(outs), axis=0).astype(v.dtype)

    return sweep_query_blocks(block, q)

def diff_attention(q, k, v, bias_table, lam, lam_init, ln_g):
    scale = DIFF_HALF ** -0.5
    s = q.shape[2]
    kpos = jnp.arange(s, dtype=jnp.int32)
    k1, k2 = k[..., :DIFF_HALF], k[..., DIFF_HALF:]

    def block(bi, qblk):
        qpos = bi * Q_BLOCK + jnp.arange(Q_BLOCK, dtype=jnp.int32)
        dist = qpos[:, None] - kpos[None, :]
        causal = dist >= 0
        bias = bias_table[t5_bucket(jnp.maximum(dist, 0))].transpose(2, 0, 1).astype(jnp.float32)

        def attn_map(qh, kh):
            l = jnp.einsum('bhqd,bhkd->bhqk', qh, kh).astype(jnp.float32) * scale + bias[None]
            return jax.nn.softmax(jnp.where(causal, l, NEG_INF), axis=-1)

        a = attn_map(qblk[..., :DIFF_HALF], k1) - lam * attn_map(qblk[..., DIFF_HALF:], k2)
        o = jnp.einsum('bhqk,bhkd->bhqd', a.astype(v.dtype), v)
        return (rms_norm(o, ln_g) * (1.0 - lam_init)).astype(v.dtype)

    return sweep_query_blocks(block, q)

def forgetting_attention(q, k, v, fg_logit):
    scale = HEAD_DIM ** -0.5
    s = q.shape[2]
    kpos = jnp.arange(s, dtype=jnp.int32)
    c = jnp.cumsum(jax.nn.log_sigmoid(fg_logit.astype(jnp.float32)), axis=-1)

    def block(bi, qblk):
        qpos = bi * Q_BLOCK + jnp.arange(Q_BLOCK, dtype=jnp.int32)
        causal = kpos[None, :] <= qpos[:, None]
        cq = lax.dynamic_slice_in_dim(c, bi * Q_BLOCK, Q_BLOCK, axis=2)
        l = jnp.einsum('bhqd,bhkd->bhqk', qblk, k).astype(jnp.float32) * scale
        l = l + cq[..., :, None] - c[..., None, :]
        p = jax.nn.softmax(jnp.where(causal, l, NEG_INF), axis=-1)
        return jnp.einsum('bhqk,bhkd->bhqd', p.astype(v.dtype), v)

    return sweep_query_blocks(block, q)

def even_mixer(h, w_in, w_out, rel_bias, lam_params, ln_g, layer):
    p = h @ w_in
    qa = split_heads(p[..., :A_WIDTH], A_HEADS)
    ka = split_heads(p[..., A_WIDTH:2 * A_WIDTH], A_HEADS)
    va = split_heads(p[..., 2 * A_WIDTH:3 * A_WIDTH], A_HEADS)
    off = 3 * A_WIDTH
    qb = split_heads(p[..., off:off + B_QK_WIDTH], B_HEADS)
    off = off + B_QK_WIDTH
    kb = split_heads(p[..., off:off + B_QK_WIDTH], B_HEADS)
    off = off + B_QK_WIDTH
    vb = split_heads(p[..., off:], B_HEADS)
    lam_init = 0.8 - 0.6 * math.exp(-0.3 * layer)
    lp = lam_params.astype(jnp.float32)
    lam = jnp.exp(jnp.sum(lp[0] * lp[1])) - jnp.exp(jnp.sum(lp[2] * lp[3])) + lam_init
    oa = dilated_attention(qa, ka, va, rel_bias[:, :A_HEADS])
    ob = diff_attention(qb, kb, vb, rel_bias[:, A_HEADS:], lam, lam_init, ln_g)
    return jnp.concatenate([oa, ob], axis=-1) @ w_out

def odd_mixer(h, w_in, b_f, w_out):
    p = h @ w_in
    q = split_heads(p[..., :C_WIDTH], C_HEADS)
    k = split_heads(p[..., C_WIDTH:2 * C_WIDTH], C_HEADS)
    v = split_heads(p[..., 2 * C_WIDTH:3 * C_WIDTH], C_HEADS)
    fg = (p[..., 3 * C_WIDTH:] + b_f).transpose(0, 2, 1)
    return forgetting_attention(q, k, v, fg) @ w_out

def peer_ffn(h, wq, subkeys, u, v):
    b, s, d = h.shape
    t = b * s
    ht = h.reshape(t, d)
    q = (ht @ wq).reshape(t, PEER_HEADS, 2, PEER_KEY_HALF)
    sc = jnp.einsum('thcd,hcnd->thcn', q, subkeys).astype(jnp.float32)
    top_s, top_i = lax.top_k(sc, PEER_TOPK)
    cand_s = (top_s[:, :, 0, :, None] + top_s[:, :, 1, None, :]).reshape(t, PEER_HEADS, -1)
    cand_i = (top_i[:, :, 0, :, None] * N_KEYS + top_i[:, :, 1, None, :]).reshape(t, PEER_HEADS, -1)
    best_s, best_j = lax.top_k(cand_s, PEER_TOPK)
    idx = jnp.take_along_axis(cand_i, best_j, axis=-1)
    gate = jax.nn.softmax(best_s, axis=-1)
    nc = t // PEER_CHUNK
    xs = (ht.reshape(nc, PEER_CHUNK, d),
          idx.reshape(nc, PEER_CHUNK, PEER_HEADS * PEER_TOPK),
          gate.reshape(nc, PEER_CHUNK, PEER_HEADS * PEER_TOPK).astype(h.dtype))

    def chunk(a):
        xc, ic, gc = a
        act = jax.nn.gelu(jnp.einsum('cd,ced->ce', xc, u[ic]), approximate=False)
        return jnp.einsum('ce,ced->cd', gc * act, v[ic])

    return lax.map(chunk, xs).reshape(b, s, d)

def setup_inputs(seed: int = 0) -> dict:
    key = jax.random.key(seed)
    ks = jax.random.split(key, 16)
    n_even = (DEPTH + 1) // 2
    n_odd = DEPTH // 2
    nrm = jax.random.normal
    f32 = jnp.float32
    return {
        'x': nrm(ks[0], (BATCH, SEQ, D_MODEL), f32),
        'norm_mix_g': 1.0 + 0.02 * nrm(ks[1], (DEPTH, D_MODEL), f32),
        'norm_ffn_g': 1.0 + 0.02 * nrm(ks[2], (DEPTH, D_MODEL), f32),
        'final_norm_g': 1.0 + 0.02 * nrm(ks[3], (D_MODEL,), f32),
        'rel_bias': 0.5 * nrm(ks[4], (N_BUCKETS, BIAS_HEADS), f32),
        'even_w_in': nrm(ks[5], (n_even, D_MODEL, EVEN_IN), f32) * D_MODEL ** -0.5,
        'even_w_out': nrm(ks[6], (n_even, EVEN_MIX, D_MODEL), f32) * EVEN_MIX ** -0.5,
        'diff_lambda': 0.1 * nrm(ks[7], (n_even, 4, DIFF_HALF), f32),
        'diff_ln_g': 1.0 + 0.02 * nrm(ks[8], (n_even, DIFF_VDIM), f32),
        'odd_w_in': nrm(ks[9], (n_odd, D_MODEL, ODD_IN), f32) * D_MODEL ** -0.5,
        'odd_b_f': FORGET_BIAS_INIT + 0.5 * nrm(ks[10], (n_odd, C_HEADS), f32),
        'odd_w_out': nrm(ks[11], (n_odd, C_WIDTH, D_MODEL), f32) * C_WIDTH ** -0.5,
        'peer_wq': nrm(ks[12], (DEPTH, D_MODEL, PEER_HEADS * 2 * PEER_KEY_HALF), f32) * D_MODEL ** -0.5,
        'peer_subkeys': nrm(ks[13], (DEPTH, PEER_HEADS, 2, N_KEYS, PEER_KEY_HALF), f32) * PEER_KEY_HALF ** -0.5,
        'peer_u': nrm(ks[14], (DEPTH, N_EXPERTS, D_MODEL), f32) * D_MODEL ** -0.5,
        'peer_v': nrm(ks[15], (DEPTH, N_EXPERTS, D_MODEL), f32) * PEER_HEADS ** -0.5,
    }

def reference(x, norm_mix_g, norm_ffn_g, final_norm_g, rel_bias, even_w_in, even_w_out,
              diff_lambda, diff_ln_g, odd_w_in, odd_b_f, odd_w_out, peer_wq, peer_subkeys,
              peer_u, peer_v):
    for layer in range(DEPTH):
        h = rms_norm(x, norm_mix_g[layer])
        i = layer // 2
        if layer % 2 == 0:
            x = x + even_mixer(h, even_w_in[i], even_w_out[i], rel_bias,
                               diff_lambda[i], diff_ln_g[i], layer)
        else:
            x = x + odd_mixer(h, odd_w_in[i], odd_b_f[i], odd_w_out[i])
        h = rms_norm(x, norm_ffn_g[layer])
        x = x + peer_ffn(h, peer_wq[layer], peer_subkeys[layer], peer_u[layer], peer_v[layer])
    return rms_norm(x, final_norm_g)


_drawn_inputs = setup_inputs


def setup_inputs(seed=0):
    import zlib

    import numpy as np

    out = dict(_drawn_inputs(seed))
    spreads = {}
    factors = {}
    for name, (base, spread) in spreads.items():
        noise = np.random.default_rng([zlib.crc32(name.encode()), seed]).standard_normal(out[name].shape)
        drawn = base * np.exp(spread * noise) if base else spread * noise
        out[name] = __import__('jax').numpy.asarray(drawn.astype(out[name].dtype))
    for name, factor in factors.items():
        out[name] = (out[name] * factor).astype(out[name].dtype)
    return out
```

```python
import math

import numpy as np
import concourse.bass as bass
from concourse import mybir
from contextlib import ExitStack

P = 128
D = 1024
KT = D // P
SEQ = 256
TT = SEQ // P
LAYERS = 2
A_HEADS, B_HEADS, C_HEADS = 8, 4, 16
BIAS_HEADS = A_HEADS + B_HEADS
BUCKETS, MAX_DISTANCE = 32, 2048
BRANCHES = ((128, 1), (512, 4), (2048, 16))
HEAD = 64
SCALE = HEAD ** -0.5
UNITS = D // P
UW = 3 * P
HEADS, TOPK, NKEYS = 8, 16, 128
HALVES = 2 * HEADS
EPS = 1e-6
LAM_INIT = 0.8 - 0.6 * math.exp(-0.3 * 0)
MASKED = -1e30
LOWEST = -3.0e38
SPAN = SEQ + P - 1
TOK_BODY = 16
TOK_HALF = 8

F32 = mybir.dt.float32
U32 = mybir.dt.uint32
ALU = mybir.AluOpType
ACT = mybir.ActivationFunctionType
AX_X = mybir.AxisListType.X


class NormSems:

    def __init__(self, sem):
        self.sq = sem("norm_sumsq")
        self.ms = sem("norm_meansq")
        self.root = sem("norm_root")
        self.hn = sem("norm_scaled")
        self.tr = sem("norm_transposed")
        self.hT = sem("norm_hT")


class LayerSems:

    def __init__(self, sem, p):
        self.w_loaded = [sem(p + "unit_w%d_loaded" % b) for b in range(2)]
        self.wo_loaded = sem(p + "w_out_loaded")
        self.qk_projected = sem(p + "qk_projected")
        self.v_projected = sem(p + "v_projected")
        self.qk_copied = sem(p + "qk_copied")
        self.v_copied = sem(p + "v_copied")
        self.scores = [sem(p + "scores%d" % m) for m in range(2)]
        self.max_ready = [sem(p + "max%d" % m) for m in range(2)]
        self.probs = [sem(p + "probs%d" % m) for m in range(2)]
        self.pt = [sem(p + "probsT%d" % m) for m in range(2)]
        self.pt_copied = [sem(p + "probsT_copied%d" % m) for m in range(2)]
        self.o_ready = sem(p + "o_ready")
        self.o_normed = sem(p + "o_normed")
        self.unit_step = sem(p + "dve_unit_steps")
        self.ln_ms = sem(p + "diff_ln_ms")
        self.ln_root = sem(p + "diff_ln_root")
        self.ocat = sem(p + "ocat_ready")
        self.o_tr = sem(p + "o_transposed")
        self.oT = sem(p + "oT_ready")
        self.mixed = sem(p + "mixer_out")
        self.x_mid = sem(p + "x_after_mixer")
        self.sk_loaded = sem(p + "subkeys_loaded")
        self.wq_loaded = [sem(p + "wq%d_loaded" % c) for c in range(2)]
        self.q_ready = [sem(p + "q%d" % c) for c in range(2)]
        self.q_copied = [sem(p + "q%d_copied" % c) for c in range(2)]
        self.sc_ready = [sem(p + "sc%d" % c) for c in range(2)]
        self.sc_read = sem(p + "sc_read")
        self.topk_step = sem(p + "dve_topk_steps")
        self.gate_d = sem(p + "gate_logits")
        self.gate_e = sem(p + "gate_exps")
        self.picked = sem(p + "picks_ready")
        self.picks_tr = sem(p + "picks_transposed")
        self.hot = sem(p + "onehots")
        self.gate_mm = sem(p + "gate_products")
        self.gate_copied = [sem(p + "gate_copied%d" % g) for g in range(2)]
        self.u_loaded = [sem(p + "u%d_loaded" % b) for b in range(2)]
        self.v_loaded = [sem(p + "v%d_loaded" % b) for b in range(2)]
        self.act_ready = sem(p + "act_ready")
        self.gelu = sem(p + "gelu_ready")
        self.weighed = sem(p + "weights_ready")
        self.summed = sem(p + "experts_summed")
        self.x_end = sem(p + "x_after_ffn")


def build(nc, a):
    with ExitStack() as ctx:
        def sb(name, shape, dt=F32):
            return ctx.enter_context(nc.sbuf_tensor(name, shape, dt))

        def sem(name):
            return ctx.enter_context(nc.semaphore(name))

        x = sb("x", [P, TT, D])
        h = sb("h", [P, TT, D])
        hT = sb("hT", [P, KT, SEQ])
        region = sb("region", [P, NKEYS * SEQ])
        expert_u = sb("expert_u", [P, 2, KT, P])
        expert_v = sb("expert_v", [P, 2, D])
        gelu_act = sb("gelu_act", [P, 2, SEQ])
        weight = sb("weight", [P, 2, SEQ])
        onehot1 = sb("onehot1", [P, TOK_HALF, P])
        onehot2 = sb("onehot2", [P, TOK_HALF, P])
        picksT = sb("picksT", [P, 3, SEQ])
        ident = sb("ident", [P, P])
        iota = sb("iota", [P, P])
        gains = sb("gains", [P, 2 * LAYERS, KT])
        sumsq = sb("sumsq", [P, TT])
        rstd = sb("rstd", [P, TT])
        lam_in = sb("lam_in", [P, 4 * HEAD])
        lam = sb("lam", [P, 4])
        neg_max = sb("neg_max", [P, 2, TT])
        denom = sb("denom", [P, 2, TT])
        rdenom = sb("rdenom", [P, 2, TT])
        ln_ss = sb("ln_ss", [P, TT * B_HEADS])
        b_f = sb("b_f", [P, C_HEADS])
        w_f = sb("w_f", [P, KT, C_HEADS])
        logsig = sb("logsig", [P, TT, C_HEADS])
        lse_tmp = sb("lse_tmp", [P, TT, C_HEADS])
        cum8 = sb("cum8", [P, TT, C_HEADS])
        ps = ctx.enter_context(nc.psum_tensor("ps", [P, 8, 512], F32))

        gate = region[:, :].rearrange("p (i t) -> p i t", i=NKEYS)
        at = [0]

        def carve(shape, like=None):
            n = int(np.prod(shape))
            v = region[:, at[0]:at[0] + n]
            at[0] += n
            assert at[0] <= NKEYS * SEQ
            if len(shape) == 1:
                return v
            names = "abcdef"[:len(shape)]
            return v.rearrange("p (%s) -> p %s" % (" ".join(names), " ".join(names)),
                               **{c: s for c, s in zip(names, shape)})

        bias8 = carve([BIAS_HEADS, SEQ])
        cumT8 = carve([C_HEADS, SEQ])
        mask8 = carve([SEQ])
        w_unit = carve([2, KT, UW])
        w_out = carve([KT, D])
        qkT = carve([2, 512])
        val = carve([2, TT, P])
        logits = carve([2, 384])
        probs = carve([2, 384])
        probsT = carve([2, 384])
        map_bias = carve([2, 384])
        tri = carve([TT, SEQ])
        ln_g = carve([P])
        row_in = carve([SPAN + 1])
        row_mask = carve([SPAN + 1])
        row_out = carve([SPAN + 1])
        cumT_row = carve([SEQ])
        o_sq = carve([TT * B_HEADS, P])
        flip = carve([P])
        hankel = carve([BIAS_HEADS, SEQ])
        at[0] = 0
        subkeys = carve([HALVES, P])
        qTs = carve([2, SEQ])
        left = carve([2, TT, P])
        cand = carve([TT, TOPK, TOPK])
        cand_left = carve([TT, TOPK, TOPK])
        head_v = carve([TT, 2, TOPK])
        head_i = carve([TT, 2, TOPK]).bitcast(U32)
        head_best = carve([TT, TOPK])
        head_j = carve([TT, TOPK]).bitcast(U32)
        top_if = carve([TT, HEADS, 2, TOPK])
        best_v = carve([TT, HEADS, TOPK])
        best_j = carve([TT, HEADS, TOPK]).bitcast(U32)
        slot_i = carve([TT * HEADS, TOPK]).bitcast(U32)
        slot_f = carve([2, TT * HEADS, TOPK])
        hit = carve([TT * HEADS, TOPK, TOPK])
        gate_z = carve([TT * HEADS])
        picks = carve([3, TT, P])

        s_const = sem("const_loaded")
        s_row = sem("row_inputs_loaded")
        s_x = sem("x_loaded")
        s_scratch = sem("bias_row_stored")
        s_bias = sem("bias_tiles_loaded")
        s_flip = sem("bias_tiles_flipped")
        s_flipped = sem("bias_tiles_ready")
        s_rowmm = sem("bias_row_product")
        s_rowdone = sem("bias_row_done")
        s_lamsum = sem("lambda_sums")
        s_lamexp = sem("lambda_exps")
        dve_straight = sem("dve_straight_steps")
        waited = sem("dve_waited_in_a_loop")
        act_straight = sem("act_straight_steps")
        s_fgw = sem("forget_weights_loaded")
        s_fg = sem("forget_logits")
        s_fgneg = sem("forget_neg_abs")
        s_fgln = sem("forget_ln")
        s_fglog = sem("forget_logsigmoid")
        s_cum = sem("forget_cumsum")
        s_cumrow = sem("forget_row_done")
        s_cumst = sem("forget_row_stored")
        s_cumld = sem("forget_tiles_loaded")
        s_fgain = sem("final_gain_loaded")
        s_y = sem("output_ready")
        s_out = sem("output_stored")

        MIX, FFN, LAST = [0, 2], [1, 3], 2 * LAYERS
        norms = NormSems(sem)
        L = [LayerSems(sem, "L%d_" % n) for n in range(LAYERS)]

        bias_row = nc.dram_tensor("bias_row", (BIAS_HEADS, SPAN), F32, kind="Internal").ap()
        cum_row = nc.dram_tensor("cum_row", (C_HEADS, SEQ), F32, kind="Internal").ap()
        bias_src = bass.AP(tensor=bias_row.tensor, offset=0, ap=[[1, P], [SPAN, BIAS_HEADS], [1, SEQ]])
        FLIP_BANKS = (0, 1, 2, 3, 6, 7)

        def free(u):
            return u + 1

        def done(u):
            return u + 2

        def credit(eng, *sems):
            for x in sems:
                eng.sem_inc(x, 1)

        def over_pairs(eng, n, body, straight=False):
            if n == 0:
                with eng.Fori(0, 2) as i:
                    body("A", i, False)
                body("B", 2, False)
                body("B", 3, True)
            else:
                with eng.Fori(0, 3) as i:
                    body("C", i, False)
                body("C", 3, True)

        block = ctx.enter_context(nc.Block())

        @block.sync
        def _(sp):
            sp.dma_start(x[:, :, :], a["x"].rearrange("b (tt p) d -> p (b tt) d", p=P)).then_inc(s_x, 16)
            sp.dma_start(row_in[0:BUCKETS, 0:SPAN], a["c_bucket"]).then_inc(s_row, 16)
            sp.dma_start(row_out[0:BUCKETS, 0:BIAS_HEADS], a["rel_bias"]).then_inc(s_row, 16)
            sp.dma_start(row_mask[0:BIAS_HEADS, 0:SPAN], a["c_rowmask"]).then_inc(s_row, 16)
            sp.dma_start(ident[:, :], a["c_ident"]).then_inc(s_const, 16)
            sp.dma_start(iota[:, :], a["c_iota"]).then_inc(s_const, 16)
            sp.dma_start(flip, a["c_flip"]).then_inc(s_const, 16)
            for n in range(LAYERS):
                sp.dma_start(gains[:, 2 * n, :], a["mix_g"][n]).then_inc(s_const, 16)
                sp.dma_start(gains[:, 2 * n + 1, :], a["ffn_g"][n]).then_inc(s_const, 16)
            sp.dma_start(lam_in[:, :], a["diff_lambda"].partition_broadcast(P)).then_inc(s_const, 16)
            sp.dma_start(ln_g, a["diff_ln_g"].partition_broadcast(P)).then_inc(s_const, 16)
            sp.dma_start(b_f[:, :], a["odd_b_f"].partition_broadcast(P)).then_inc(s_const, 16)
            sp.dma_start(w_f[:, :, :], a["w_f"]).then_inc(s_const, 16)
            for n in range(LAYERS):
                s = L[n]
                if n > 0:
                    sp.wait_ge(L[n - 1].weighed, free(NKEYS))
                    sp.dma_start(tri, a["c_tri"]).then_inc(s_fgw, 16)
                    sp.dma_start(mask8, a["c_mask8"]).then_inc(s_fgw, 16)
                for b in range(2):
                    sp.dma_start(w_unit[:, b], a["w_unit"][n, b]).then_inc(s.w_loaded[b], 16)
                sp.dma_start(w_out, a["w_out"][n]).then_inc(s.wo_loaded, 16)
                if n == 0:
                    sp.wait_ge(s_rowdone, 1)
                    sp.dma_start(bias_row, row_out[0:BIAS_HEADS, 0:SPAN]).then_inc(s_scratch, 16)
                    sp.wait_ge(s_scratch, 16)
                    sp.dma_start(hankel, bias_src).then_inc(s_bias, 16)
                else:
                    sp.wait_ge(s_cumrow, 1)
                    sp.dma_start(cum_row, cumT_row[0:C_HEADS, :]).then_inc(s_cumst, 16)
                    sp.wait_ge(s_cumst, 16)
                    sp.dma_start(cumT8, cum_row.rearrange("h t -> (h t)").partition_broadcast(P)
                                 .rearrange("p (h t) -> p h t", h=C_HEADS)).then_inc(s_cumld, 16)
                with sp.Fori(1, UNITS // 2) as i:
                    for b in range(2):
                        sp.wait_ge(s.v_projected, 2 * i + b - 1)
                        sp.dma_start(w_unit[:, b], a["w_unit"][n, 2 * i + b]).then_inc(s.w_loaded[b], 16)
                for c in range(2):
                    sp.dma_start(expert_u[:, c], a["w_query"][n, c]).then_inc(s.wq_loaded[c], 16)
                sp.wait_ge(s.mixed, 1)
                sp.wait_ge(s.x_mid, 2)
                sp.dma_start(subkeys, a["subkeys"][n]).then_inc(s.sk_loaded, 16)
                with sp.Fori(1, HEADS) as i:
                    for c in range(2):
                        sp.wait_ge(s.q_ready[c], i)
                        sp.dma_start(expert_u[:, c], a["w_query"][n, 2 * i + c]).then_inc(s.wq_loaded[c], 16)
                for b in range(2):
                    sp.wait_ge(s.q_ready[b], HEADS)
                    sp.dma_start(expert_u[:, b], a["peer_u"][n, b]).then_inc(s.u_loaded[b], 16)
                    sp.dma_start(expert_v[:, b, :], a["peer_v"][n][:, b, :]).then_inc(s.v_loaded[b], 16)
                with sp.Fori(1, NKEYS // 2) as i:
                    for b in range(2):
                        sp.wait_ge(s.act_ready, 2 * i + b - 1)
                        sp.dma_start(expert_u[:, b], a["peer_u"][n, 2 * i + b]).then_inc(s.u_loaded[b], 16)
                        sp.wait_ge(s.summed, 2 * i + b - 1)
                        sp.dma_start(expert_v[:, b, :], a["peer_v"][n][:, 2 * i + b, :]).then_inc(s.v_loaded[b], 16)
            sp.wait_ge(L[-1].summed, NKEYS)
            sp.dma_start(expert_v[:, 0, :], a["final_g"].partition_broadcast(P)).then_inc(s_fgain, 16)
            sp.wait_ge(s_y, 1)
            sp.dma_start(a["y"].rearrange("b (tt p) d -> p (b tt) d", p=P), h[:, :, :]).then_inc(s_out, 16)
            sp.wait_ge(s_out, 16)

        @block.tensor
        def _(pe):
            def turn(ready, ready_at, done):
                pe.wait_ge(ready, ready_at)
                for kt in range(KT):
                    for tt in range(TT):
                        c = (kt % 2) * SEQ + tt * P
                        last = pe.transpose(ps[:, kt // 2, c:c + P], h[:, tt, kt * P:(kt + 1) * P], ident[:, :])
                    if kt % 2:
                        last.then_inc(done, 1)

            def project_unit(s, b, u, i):
                pe.wait_ge(s.w_loaded[b], 16 * (i + 1))
                pe.wait_ge(s.qk_copied, free(u))
                for part in range(2):
                    for kt in range(KT):
                        last = pe.matmul(ps[:, 4, part * SEQ:(part + 1) * SEQ],
                                         w_unit[:, b, kt, part * P:(part + 1) * P], hT[:, kt, :],
                                         start=(kt == 0), stop=(kt == KT - 1))
                last.then_inc(s.qk_projected, 1)
                pe.wait_ge(s.v_copied, free(u))
                for tt in range(TT):
                    for kt in range(KT):
                        last = pe.matmul(ps[:, 5, tt * P:(tt + 1) * P], hT[:, kt, tt * P:(tt + 1) * P],
                                         w_unit[:, b, kt, 2 * P:3 * P], start=(kt == 0), stop=(kt == KT - 1))
                last.then_inc(s.v_projected, 1)

            def attend(s, kind, b, u):
                pe.wait_ge(s.qk_copied, done(u))
                for m in range(2):
                    r = slice(m * HEAD, (m + 1) * HEAD)
                    pe.wait_ge(s.pt_copied[m], free(u))
                    pe.matmul(ps[:, 6 + m, 0:P], qkT[r, b, 0:P], qkT[r, b, SEQ:SEQ + P], start=True, stop=True)
                    pe.matmul(ps[:, 6 + m, P:3 * P], qkT[r, b, P:SEQ], qkT[r, b, SEQ:2 * SEQ],
                              start=True, stop=True).then_inc(s.scores[m], 1)

            def combine(s, kind, b, u):
                for m in range(2):
                    pe.wait_ge(s.probs[m], done(u))
                    for blk in range(3):
                        last = pe.transpose(ps[:, 6 + m, blk * P:(blk + 1) * P],
                                            probs[:, m, blk * P:(blk + 1) * P], ident[:, :])
                    last.then_inc(s.pt[m], 1)
                pe.wait_ge(s.v_copied, done(u))
                pe.wait_ge(s.o_normed, free(u))
                w = P if kind == "B" else HEAD
                for m in range(2):
                    pe.wait_ge(s.pt_copied[m], done(u))
                    v0 = 0 if kind == "B" else m * HEAD
                    out = [ps[:, 0, (tt * 2 + m) * w:(tt * 2 + m + 1) * w] for tt in range(TT)]
                    pe.matmul(out[0], probsT[:, m, 0:P], val[:, b, 0, v0:v0 + w], start=True, stop=True)
                    pe.matmul(out[1], probsT[:, m, P:2 * P], val[:, b, 0, v0:v0 + w], start=True, stop=False)
                    last = pe.matmul(out[1], probsT[:, m, 2 * P:3 * P], val[:, b, 1, v0:v0 + w],
                                     start=False, stop=True)
                last.then_inc(s.o_ready, 1)

            for s in L:
                credit(pe, *s.pt, *s.sc_ready)

            pe.wait_ge(s_row, 48)
            pe.matmul(ps[0:BIAS_HEADS, 5, 0:SPAN], row_out[0:BUCKETS, 0:BIAS_HEADS], row_in[0:BUCKETS, 0:SPAN],
                      start=True, stop=True).then_inc(s_rowmm, 1)
            pe.wait_ge(s_const, 16 * (7 + 2 * LAYERS))
            for n in range(LAYERS):
                s = L[n]
                turn(norms.hn, TT * (MIX[n] + 1), norms.tr)
                pe.wait_ge(norms.hT, KT * (MIX[n] + 1))
                if n == 0:
                    pe.wait_ge(s_rowdone, 1)
                if n == 1:
                    for tt in range(TT):
                        for kt in range(KT):
                            last = pe.matmul(ps[:, 2, tt * C_HEADS:(tt + 1) * C_HEADS],
                                             hT[:, kt, tt * P:(tt + 1) * P], w_f[:, kt, :],
                                             start=(kt == 0), stop=(kt == KT - 1))
                    last.then_inc(s_fg, 1)
                project_unit(s, 0, 0, 0)
                if n == 0:
                    pe.wait_ge(s_bias, 16)
                    for j, bank in enumerate(FLIP_BANKS):
                        last = pe.matmul(ps[:, bank, :], flip,
                                         hankel[:, 2 * j:2 * j + 2, :].rearrange("p h k -> p (h k)"),
                                         start=True, stop=True)
                    last.then_inc(s_flip, 1)
                    pe.wait_ge(s_flipped, len(FLIP_BANKS))
                if n == 1:
                    pe.wait_ge(s_fglog, 1)
                    pe.wait_ge(s_fgw, 32)
                    for tt in range(TT):
                        for kt in range(TT):
                            pe.matmul(ps[:, 2, tt * C_HEADS:(tt + 1) * C_HEADS], tri[:, kt, tt * P:(tt + 1) * P],
                                      logsig[:, kt, :], start=(kt == 0), stop=(kt == TT - 1))
                    for kt in range(TT):
                        last = pe.matmul(ps[0:C_HEADS, 3, 0:SEQ], logsig[:, kt, :], tri[:, kt, :],
                                         start=(kt == 0), stop=(kt == TT - 1))
                    last.then_inc(s_cum, 1)

                def pair(kind, i, last_pair):
                    for b in range(2):
                        u = 2 * i + b
                        attend(s, kind, b, u)
                        if not (last_pair and b):
                            project_unit(s, 1 - b, u + 1, i + b)
                        combine(s, kind, b, u)

                over_pairs(pe, n, pair)

                turn(*((s.ocat, 1) if n == 0 else (s.o_normed, free(UNITS))), s.o_tr)
                pe.wait_ge(s.oT, KT)
                pe.wait_ge(s.wo_loaded, 16)
                for tt in range(TT):
                    for half in range(2):
                        for kt in range(KT):
                            last = pe.matmul(ps[:, 4 + 2 * tt + half, :], hT[:, kt, tt * P:(tt + 1) * P],
                                             w_out[:, kt, half * 512:(half + 1) * 512],
                                             start=(kt == 0), stop=(kt == KT - 1))
                    last.then_inc(s.mixed, 1)

                turn(norms.hn, TT * (FFN[n] + 1), norms.tr)
                pe.wait_ge(norms.hT, KT * (FFN[n] + 1))
                pe.wait_ge(s.sk_loaded, 16)
                with pe.Fori(0, HEADS) as i:
                    for c in range(2):
                        pe.wait_ge(s.wq_loaded[c], 16 * (i + 1))
                        pe.wait_ge(s.q_copied[c], free(i))
                        for kt in range(KT):
                            last = pe.matmul(ps[:, 4 + c, 0:SEQ], expert_u[:, c, kt, :], hT[:, kt, :],
                                             start=(kt == 0), stop=(kt == KT - 1))
                        last.then_inc(s.q_ready[c], 1)
                    for c in range(2):
                        pe.wait_ge(s.q_copied[c], done(i))
                        if c == 0:
                            pe.wait_ge(s.sc_read, free(i))
                        for tt in range(TT):
                            last = pe.matmul(ps[:, 6 + c, tt * P:(tt + 1) * P], qTs[:, c, tt * P:(tt + 1) * P],
                                             subkeys[:, 2 * i + c, :], start=True, stop=True)
                        last.then_inc(s.sc_ready[c], 1)

                pe.wait_ge(s.picked, 1)
                for w in range(3):
                    for tt in range(TT):
                        c = w * SEQ + tt * P
                        last = pe.transpose(ps[:, c // 512, c % 512:c % 512 + P], picks[:, w, tt, :], ident[:, :])
                last.then_inc(s.picks_tr, 1)

                with pe.Fori(0, SEQ // TOK_BODY) as i:
                    for g in range(2):
                        pe.wait_ge(s.gate_copied[g], free(i))
                        for j in range(TOK_HALF):
                            pe.wait_ge(s.hot, TOK_BODY * i + TOK_HALF * g + j + 1)
                            pe.matmul(ps[:, 2 * g + j // 4, (j % 4) * P:(j % 4 + 1) * P], onehot1[:, j, :],
                                      onehot2[:, j, :], start=True, stop=True).then_inc(s.gate_mm, 1)

                for g in range(2):
                    pe.wait_ge(s.gate_copied[g], free(SEQ // TOK_BODY))
                for tt in range(TT):
                    for half in range(2):
                        pe.matmul(ps[:, 2 * tt + half, :], ident[:, :], x[:, tt, half * 512:(half + 1) * 512],
                                  start=True, stop=False)

                def experts_in(b, c, i):
                    pe.wait_ge(s.u_loaded[b], 16 * (i + 1))
                    for kt in range(KT):
                        last = pe.matmul(ps[:, 4 + b, 0:SEQ], expert_u[:, b, kt, :], hT[:, kt, :],
                                         start=(kt == 0), stop=(kt == KT - 1))
                    last.then_inc(s.act_ready, 1)

                def experts_out(b, c, i, stop):
                    pe.wait_ge(s.weighed, done(c))
                    pe.wait_ge(s.v_loaded[b], 16 * (i + 1))
                    for tt in range(TT):
                        for half in range(2):
                            last = pe.matmul(ps[:, 2 * tt + half, :], weight[:, b, tt * P:(tt + 1) * P],
                                             expert_v[:, b, half * 512:(half + 1) * 512], start=False, stop=stop)
                    last.then_inc(s.summed, 1)

                experts_in(0, 0, 0)
                with pe.Fori(0, NKEYS // 2 - 1) as i:
                    experts_in(1, 2 * i + 1, i)
                    experts_out(0, 2 * i, i, False)
                    experts_in(0, 2 * i + 2, i + 1)
                    experts_out(1, 2 * i + 1, i, False)
                i = NKEYS // 2 - 1
                experts_in(1, 2 * i + 1, i)
                experts_out(0, 2 * i, i, False)
                experts_out(1, 2 * i + 1, i, True)

        @block.scalar
        def _(act):
            for s in L:
                credit(act, s.qk_copied, s.v_copied, *s.probs, *s.q_copied, *s.gate_copied)

            def norm(k, ready, ready_at):
                act.wait_ge(ready, ready_at)
                for tt in range(TT):
                    act.activation(h[:, tt, :], x[:, tt, :], ACT.Square, accum_out=sumsq[:, tt:tt + 1]).then_inc(norms.sq, 1)
                act.wait_ge(norms.ms, k + 1)
                act.activation(rstd[:, :], sumsq[:, :], ACT.Sqrt).then_inc(norms.root, 1)

            for n in range(LAYERS):
                s = L[n]
                if n == 0:
                    norm(MIX[0], s_x, 16)
                    act.wait_ge(s_lamsum, 1)
                    act.activation(lam[:, 2:4], lam[:, 0:2], ACT.Exp).then_inc(s_lamexp, 1)
                else:
                    norm(MIX[n], L[n - 1].x_end, 2)
                    act.wait_ge(s_fgneg, 1)
                    act.activation(lse_tmp[:, :, :], lse_tmp[:, :, :], ACT.Exp).then_inc(act_straight, 1)
                    act.wait_ge(s_fgneg, 2)
                    act.activation(lse_tmp[:, :, :], lse_tmp[:, :, :], ACT.Ln).then_inc(s_fgln, 1)

                def copy_unit(b, u):
                    act.wait_ge(s.qk_projected, u + 1)
                    act.copy(qkT[:, b, :], ps[:, 4, :]).then_inc(s.qk_copied, 1)
                    act.wait_ge(s.v_projected, u + 1)
                    act.copy(val[:, b, :, :], ps[:, 5, 0:TT * P].rearrange("p (t c) -> p t c", t=TT))\
                       .then_inc(s.v_copied, 1)

                def pair(kind, i, last_pair):
                    for b in range(2):
                        u = 2 * i + b
                        for m in range(2):
                            act.wait_ge(s.max_ready[m], u + 1)
                            act.wait_ge(s.pt[m], free(u))
                            act.wait_ge(s.o_normed, free(u))
                            act.activation(probs[:, m, 0:P], logits[:, m, 0:P], ACT.Exp,
                                           bias=neg_max[:, m, 0:1], scale=-1.0, accum_out=denom[:, m, 0:1])
                            act.activation(probs[:, m, P:3 * P], logits[:, m, P:3 * P], ACT.Exp,
                                           bias=neg_max[:, m, 1:2], scale=-1.0, accum_out=denom[:, m, 1:2])\
                               .then_inc(s.probs[m], 1)
                        if not (last_pair and b):
                            copy_unit(1 - b, u + 1)

                copy_unit(0, 0)
                over_pairs(act, n, pair)
                if n == 0:
                    act.wait_ge(s.ln_ms, 1)
                    act.activation(ln_ss[:, :], ln_ss[:, :], ACT.Sqrt).then_inc(s.ln_root, 1)
                norm(FFN[n], s.x_mid, 2)

                with act.Fori(0, HEADS) as i:
                    for c in range(2):
                        act.wait_ge(s.q_ready[c], i + 1)
                        act.wait_ge(s.sc_ready[c], free(i))
                        act.copy(qTs[:, c, :], ps[:, 4 + c, 0:SEQ]).then_inc(s.q_copied[c], 1)
                act.wait_ge(s.gate_d, 1)
                act.activation(best_v, best_v, ACT.Exp).then_inc(s.gate_e, 1)

                act.wait_ge(s.hot, 1)
                with act.Fori(0, SEQ // TOK_BODY) as i:
                    for g in range(2):
                        act.wait_ge(s.gate_mm, TOK_BODY * i + TOK_HALF * (g + 1))
                        act.copy(gate[:, :, bass.ds(TOK_BODY * i + TOK_HALF * g, TOK_HALF)],
                                 ps[:, 2 * g:2 * g + 2, :].rearrange("p b (t i) -> p i (b t)", t=4))\
                           .then_inc(s.gate_copied[g], 1)

                with act.Fori(0, NKEYS // 2) as i:
                    for b in range(2):
                        act.wait_ge(s.act_ready, 2 * i + b + 1)
                        act.wait_ge(s.weighed, free(2 * i))
                        act.activation(gelu_act[:, b, :], ps[:, 4 + b, 0:SEQ], ACT.Gelu).then_inc(s.gelu, 1)
                act.wait_ge(s.summed, NKEYS)
                for half in range(2):
                    last = act.copy(x[:, 1, half * 512:(half + 1) * 512], ps[:, 2 + half, :])
                last.then_inc(s.x_end, 1)
            norm(LAST, L[-1].x_end, 2)

        @block.vector
        def _(dve):
            straight = [0]

            def then(ins):
                straight[0] += 1
                ins.then_inc(dve_straight, 1)
                dve.wait_ge(dve_straight, straight[0])

            def wait_apart(sem, value):
                dve.wait_ge(sem, value)
                dve.sem_inc(waited, 1)

            class Steps:

                def __init__(self, sem, turns, per):
                    self.sem, self.base, self.n = sem, turns * per, 0

                def add(self, ins):
                    self.n += 1
                    ins.then_inc(self.sem, 1)
                    return self.n

                def wait(self, k):
                    wait_apart(self.sem, self.base + k)

            def norm_scale(k):
                dve.wait_ge(norms.sq, TT * (k + 1))
                dve.tensor_scalar(sumsq[:, :], sumsq[:, :], 1.0 / D, EPS, ALU.mult, ALU.add).then_inc(norms.ms, 1)
                dve.wait_ge(norms.root, k + 1)
                then(dve.reciprocal(rstd[:, :], rstd[:, :]))

            def norm(k):
                norm_scale(k)
                for tt in range(TT):
                    dve.tensor_scalar(h[:, tt, :], x[:, tt, :], rstd[:, tt:tt + 1], None, ALU.mult).then_inc(norms.hn, 1)
                for kt in range(KT):
                    if kt % 2 == 0:
                        dve.wait_ge(norms.tr, KT // 2 * k + kt // 2 + 1)
                    dve.tensor_scalar(hT[:, kt, :], ps[:, kt // 2, (kt % 2) * SEQ:(kt % 2 + 1) * SEQ],
                                      gains[:, k, kt:kt + 1], None, ALU.mult).then_inc(norms.hT, 1)

            for s in L:
                credit(dve, *s.pt_copied, s.o_normed, s.sc_read, s.weighed)

            dve.wait_ge(s_rowmm, 1)
            then(dve.tensor_tensor(row_mask[0:BIAS_HEADS, 0:SPAN], ps[0:BIAS_HEADS, 5, 0:SPAN],
                                   row_mask[0:BIAS_HEADS, 0:SPAN], ALU.add))
            dve.tensor_scalar(row_out[0:BIAS_HEADS, 0:SPAN], row_mask[0:BIAS_HEADS, 0:SPAN], 1.0 / SCALE, None,
                              ALU.mult).then_inc(s_rowdone, 1)
            dve.wait_ge(s_const, 16 * (7 + 2 * LAYERS))
            for j in range(2):
                last = dve.tensor_tensor_reduce(lam_in[:, 2 * j * HEAD:(2 * j + 1) * HEAD],
                                                lam_in[:, 2 * j * HEAD:(2 * j + 1) * HEAD],
                                                lam_in[:, (2 * j + 1) * HEAD:(2 * j + 2) * HEAD], 1.0, 0.0,
                                                ALU.mult, ALU.add, lam[:, j:j + 1])
            last.then_inc(s_lamsum, 1)

            for n in range(LAYERS):
                s = L[n]
                norm(MIX[n])
                if n == 0:
                    dve.wait_ge(s_lamexp, 1)
                    then(dve.tensor_tensor(lam[:, 0:1], lam[:, 3:4], lam[:, 2:3], ALU.subtract))
                    then(dve.tensor_scalar(lam[:, 0:1], lam[:, 0:1], -LAM_INIT, None, ALU.add))
                    then(dve.tensor_scalar(ln_g, ln_g, 1.0 - LAM_INIT, None, ALU.mult))
                    dve.wait_ge(s_flip, 1)
                    for j, bank in enumerate(FLIP_BANKS):
                        dve.tensor_copy(bias8[:, 2 * j:2 * j + 2, :],
                                        ps[:, bank, :].rearrange("p (h k) -> p h k", h=2)).then_inc(s_flipped, 1)
                    dve.wait_ge(s_flipped, len(FLIP_BANKS))
                else:
                    dve.wait_ge(s_fg, 1)
                    fg = ps[:, 2, 0:TT * C_HEADS].rearrange("p (t h) -> p t h", t=TT)
                    for tt in range(TT):
                        ins = dve.tensor_tensor(logsig[:, tt, :], fg[:, tt, :], b_f[:, :], ALU.add)
                    then(ins)
                    dve.scalar_tensor_tensor(lse_tmp[:, :, :], logsig[:, :, :], -1.0, logsig[:, :, :], ALU.mult, ALU.min)\
                       .then_inc(s_fgneg, 1)
                    then(dve.tensor_scalar(logsig[:, :, :], logsig[:, :, :], 0.0, None, ALU.min))
                    dve.wait_ge(act_straight, 1)
                    dve.tensor_scalar(lse_tmp[:, :, :], lse_tmp[:, :, :], 1.0, None, ALU.add).then_inc(s_fgneg, 1)
                    dve.wait_ge(s_fgln, 1)
                    dve.tensor_tensor(logsig[:, :, :], logsig[:, :, :], lse_tmp[:, :, :], ALU.subtract)\
                       .then_inc(s_fglog, 1)
                    dve.wait_ge(s_cum, 1)
                    dve.tensor_scalar(cumT_row[0:C_HEADS, :], ps[0:C_HEADS, 3, 0:SEQ], -1.0 / SCALE, None,
                                      ALU.mult).then_inc(s_cumrow, 1)
                    then(dve.tensor_scalar(cum8[:, :, :], fg, 1.0 / SCALE, None, ALU.mult))
                    dve.wait_ge(s_fgw, 32)
                    dve.wait_ge(s_cumld, 16)

                steps_per_unit = {"A": 3, "B": 5, "C": 3}

                def pair(kind, i, last_pair):
                    st = Steps(s.unit_step, i if kind != "B" else i, 2 * steps_per_unit[kind])
                    if kind == "B":
                        st.base = 4 * steps_per_unit["A"] + (i - 2) * 2 * steps_per_unit["B"]
                    for b in range(2):
                        u = 2 * i + b
                        for m in range(2):
                            if kind == "C":
                                hd = 2 * u + m
                                dve.scalar_tensor_tensor(map_bias[:, m, 0:P], cumT8[:, hd, 0:P], cum8[:, 0, bass.ds(hd, 1)],
                                                         mask8[:, P:SEQ], ALU.add, ALU.add)
                                k = st.add(dve.scalar_tensor_tensor(map_bias[:, m, P:3 * P], cumT8[:, hd, :],
                                                                    cum8[:, 1, bass.ds(hd, 1)],
                                                                    mask8, ALU.add, ALU.add))
                                t0 = map_bias[:, m, 0:P]
                            else:
                                hd = 2 * u + m if kind == "A" else A_HEADS + u - A_HEADS // 2
                                k = st.add(dve.tensor_copy(map_bias[:, m, P:3 * P], bias8[:, hd, :]))
                                t0 = map_bias[:, m, 2 * P:3 * P]
                            t1 = map_bias[:, m, P:3 * P]
                            st.wait(k)
                            dve.wait_ge(s.scores[m], u + 1)
                            wait_apart(s.probs[m], free(u))
                            dve.tensor_tensor_reduce(logits[:, m, 0:P], ps[:, 6 + m, 0:P], t0, -SCALE, -LOWEST,
                                                     ALU.add, ALU.min, neg_max[:, m, 0:1])
                            dve.tensor_tensor_reduce(logits[:, m, P:3 * P], ps[:, 6 + m, P:3 * P], t1, -SCALE,
                                                     -LOWEST, ALU.add, ALU.min, neg_max[:, m, 1:2])\
                               .then_inc(s.max_ready[m], 1)
                        for m in range(2):
                            dve.wait_ge(s.pt[m], done(u))
                            dve.tensor_copy(probsT[:, m, :], ps[:, 6 + m, 0:3 * P]).then_inc(s.pt_copied[m], 1)
                        k = st.add(dve.reciprocal(rdenom[:, :, :], denom[:, :, :]))
                        st.wait(k)
                        dve.wait_ge(s.o_ready, u + 1)
                        if kind == "B":
                            k = st.add(dve.tensor_scalar(rdenom[:, 1, :], rdenom[:, 1, :], lam[:, 0:1], None, ALU.mult))
                            st.wait(k)
                            hu = h[:, :, :].rearrange("p t (u c) -> p t u c", u=UNITS)[:, :, u, :]
                            for tt in range(TT):
                                ins = dve.tensor_scalar(hu[:, tt, :], ps[:, 0, tt * 2 * P:(tt * 2 + 1) * P],
                                                        rdenom[:, 0, tt:tt + 1], None, ALU.mult)
                            k = st.add(ins)
                            st.wait(k)
                            for tt in range(TT):
                                ins = dve.scalar_tensor_tensor(hu[:, tt, :], ps[:, 0, (tt * 2 + 1) * P:(tt * 2 + 2) * P],
                                                               rdenom[:, 1, tt:tt + 1], hu[:, tt, :], ALU.mult, ALU.add)
                        else:
                            hu = h[:, :, :].rearrange("p t (u m c) -> p t u m c", u=UNITS, m=2)
                            for m in range(2):
                                for tt in range(TT):
                                    ins = dve.tensor_scalar(hu[:, tt, u, m, :],
                                                            ps[:, 0, (tt * 2 + m) * HEAD:(tt * 2 + m + 1) * HEAD],
                                                            rdenom[:, m, tt:tt + 1], None, ALU.mult)
                        ins.then_inc(s.o_normed, 1)
                    assert st.n == 2 * steps_per_unit[kind]

                over_pairs(dve, n, pair)
                if n == 0:
                    dve.wait_ge(s.o_normed, free(UNITS))
                    ob = h[:, :, :].rearrange("p t (u c) -> p t u c", u=UNITS)
                    for tt in range(TT):
                        for b in range(B_HEADS):
                            j = tt * B_HEADS + b
                            ins = dve.tensor_tensor_reduce(o_sq[:, j, :], ob[:, tt, 4 + b, :], ob[:, tt, 4 + b, :], 1.0, 0.0,
                                                           ALU.mult, ALU.add, ln_ss[:, j:j + 1])
                    then(ins)
                    dve.tensor_scalar(ln_ss[:, :], ln_ss[:, :], 1.0 / P, EPS, ALU.mult, ALU.add).then_inc(s.ln_ms, 1)
                    dve.wait_ge(s.ln_root, 1)
                    then(dve.reciprocal(ln_ss[:, :], ln_ss[:, :]))
                    for tt in range(TT):
                        for b in range(B_HEADS):
                            j = tt * B_HEADS + b
                            ins = dve.scalar_tensor_tensor(ob[:, tt, 4 + b, :], ob[:, tt, 4 + b, :], ln_ss[:, j:j + 1],
                                                           ln_g, ALU.mult, ALU.mult)
                    ins.then_inc(s.ocat, 1)
                for bank in range(KT // 2):
                    dve.wait_ge(s.o_tr, bank + 1)
                    dve.tensor_copy(hT[:, 2 * bank:2 * bank + 2, :],
                                    ps[:, bank, :].rearrange("p (k t) -> p k t", k=2)).then_inc(s.oT, 2)
                for tt in range(TT):
                    dve.wait_ge(s.mixed, tt + 1)
                    for half in range(2):
                        xs = x[:, tt, half * 512:(half + 1) * 512]
                        ins = dve.tensor_tensor(xs, ps[:, 4 + 2 * tt + half, :], xs, ALU.add)
                    ins.then_inc(s.x_mid, 1)
                norm(FFN[n])

                per = 4 * 4 + 2 + 2 * 4 + 3

                with dve.Fori(0, HEADS) as i:
                    st = Steps(s.topk_step, i, per)
                    lanes = [(tt, c) for c in range(2) for tt in range(TT)]
                    top = {j: head_v[:, j[0], j[1], :] for j in lanes}
                    idx = {j: head_i[:, j[0], j[1], :] for j in lanes}
                    src = {j: ps[:, 6 + j[1], j[0] * P:(j[0] + 1) * P] for j in lanes}
                    k1, k2, k3 = {}, {}, {}
                    for j in lanes:
                        if j[0] == 0:
                            wait_apart(s.sc_ready[j[1]], done(i))
                        k1[j] = st.add(dve.max(top[j][:, 0:8], src[j]))
                    for j in lanes:
                        st.wait(k1[j])
                        k2[j] = st.add(dve.match_replace(left[:, j[1], j[0], :], top[j][:, 0:8], src[j], LOWEST))
                        ins = dve.max_index(idx[j][:, 0:8], top[j][:, 0:8], src[j])
                    ins.then_inc(s.sc_read, 1)
                    for j in lanes:
                        st.wait(k2[j])
                        k3[j] = st.add(dve.max(top[j][:, 8:16], left[:, j[1], j[0], :]))
                    for j in lanes:
                        st.wait(k3[j])
                        last = st.add(dve.max_index(idx[j][:, 8:16], top[j][:, 8:16], left[:, j[1], j[0], :]))
                    st.wait(last)
                    kc = {}
                    for tt in range(TT):
                        kc[tt] = st.add(dve.tensor_tensor(cand[:, tt],
                                                          top[tt, 0].unsqueeze(2).to_broadcast([P, TOPK, TOPK]),
                                                          top[tt, 1].unsqueeze(1).to_broadcast([P, TOPK, TOPK]), ALU.add))
                    flat = [cand[:, tt].rearrange("p a b -> p (a b)") for tt in range(TT)]
                    rest = [cand_left[:, tt].rearrange("p a b -> p (a b)") for tt in range(TT)]
                    best = [head_best[:, tt, :] for tt in range(TT)]
                    bidx = [head_j[:, tt, :] for tt in range(TT)]
                    for tt in range(TT):
                        st.wait(kc[tt])
                        k1[tt] = st.add(dve.max(best[tt][:, 0:8], flat[tt]))
                    for tt in range(TT):
                        st.wait(k1[tt])
                        dve.max_index(bidx[tt][:, 0:8], best[tt][:, 0:8], flat[tt])
                        k2[tt] = st.add(dve.match_replace(rest[tt], best[tt][:, 0:8], flat[tt], LOWEST))
                    for tt in range(TT):
                        st.wait(k2[tt])
                        k3[tt] = st.add(dve.max(best[tt][:, 8:16], rest[tt]))
                    for tt in range(TT):
                        st.wait(k3[tt])
                        ins = dve.max_index(bidx[tt][:, 8:16], best[tt][:, 8:16], rest[tt])
                        last = st.add(ins)
                    st.add(dve.tensor_copy(top_if[:, :, i, :, :], head_i))
                    st.add(dve.tensor_copy(best_v[:, :, i, :], head_best))
                    st.wait(last)
                    st.add(dve.tensor_copy(best_j[:, :, i, :], head_j))
                    assert st.n == per, st.n
                dve.wait_ge(s.topk_step, HEADS * per)

                groups = TT * HEADS
                bv = best_v.rearrange("p t h k -> p (t h) k")
                gate_out = picks[:, 2].rearrange("p t (h k) -> p (t h) k", h=HEADS)
                then(dve.tensor_tensor(gate_out, bv, bv[:, :, 0:1].to_broadcast([P, groups, TOPK]), ALU.subtract))
                dve.tensor_copy(bv, gate_out).then_inc(s.gate_d, 1)
                for c in range(2):
                    bj = best_j.rearrange("p t h k -> p (t h) k")
                    if c == 0:
                        then(dve.tensor_scalar(slot_i, bj, 4, None, ALU.logical_shift_right))
                    else:
                        then(dve.tensor_scalar(slot_i, bj, TOPK - 1, None, ALU.bitwise_and))
                    then(dve.tensor_copy(slot_f[:, c], slot_i))
                    then(dve.tensor_tensor(hit, slot_f[:, c].unsqueeze(3).to_broadcast([P, groups, TOPK, TOPK]),
                                           iota[:, 0:TOPK].unsqueeze(1).unsqueeze(1).to_broadcast([P, groups, TOPK, TOPK]),
                                           ALU.is_equal))
                    then(dve.tensor_tensor(hit, hit, top_if.rearrange("p t h c k -> p (t h) c k")[:, :, c, :].unsqueeze(2).to_broadcast([P, groups, TOPK, TOPK]),
                                           ALU.mult))
                    dve.tensor_reduce(picks[:, c].rearrange("p t (h k) -> p (t h) k", h=HEADS), hit, AX_X, ALU.add)
                dve.wait_ge(s.gate_e, 1)
                then(dve.tensor_reduce(gate_z, bv, AX_X, ALU.add))
                then(dve.reciprocal(gate_z, gate_z))
                dve.tensor_tensor(gate_out, bv, gate_z.unsqueeze(2).to_broadcast([P, groups, TOPK]),
                                  ALU.mult).then_inc(s.picked, 1)
                dve.wait_ge(s.picks_tr, 1)
                then(dve.tensor_copy(picksT[:, :, :].rearrange("p w t -> p (w t)"),
                                     ps[:, 0:2, :].rearrange("p b c -> p (b c)")[:, 0:3 * SEQ]))

                with dve.Fori(0, SEQ // TOK_BODY) as i:
                    for g in range(2):
                        for j in range(TOK_HALF):
                            t = TOK_BODY * i + TOK_HALF * g + j
                            if g:
                                dve.wait_ge(s.gate_mm, TOK_BODY * i + j + 1)
                            else:
                                dve.wait_ge(s.gate_copied[1], free(i))
                            dve.tensor_scalar(onehot1[:, j, :], iota[:, :], picksT[:, 0, bass.ds(t, 1)],
                                              picksT[:, 2, bass.ds(t, 1)], ALU.is_equal, ALU.mult)
                            dve.tensor_scalar(onehot2[:, j, :], iota[:, :], picksT[:, 1, bass.ds(t, 1)],
                                              None, ALU.is_equal).then_inc(s.hot, 1)

                for g in range(2):
                    dve.wait_ge(s.gate_copied[g], free(SEQ // TOK_BODY))
                with dve.Fori(0, NKEYS // 2) as i:
                    for b in range(2):
                        dve.wait_ge(s.gelu, 2 * i + b + 1)
                        dve.tensor_tensor(weight[:, b, :], gelu_act[:, b, :], gate[:, 2 * i + b, :],
                                          ALU.mult).then_inc(s.weighed, 1)
                dve.wait_ge(s.summed, NKEYS)
                for half in range(2):
                    last = dve.tensor_copy(x[:, 0, half * 512:(half + 1) * 512], ps[:, half, :])
                last.then_inc(s.x_end, 1)

            norm_scale(LAST)
            dve.wait_ge(s_fgain, 16)
            for tt in range(TT):
                ins = dve.scalar_tensor_tensor(h[:, tt, :], x[:, tt, :], rstd[:, tt:tt + 1], expert_v[:, 0, :],
                                               ALU.mult, ALU.mult)
            ins.then_inc(s_y, 1)


def _t5_bucket(dist):
    exact = BUCKETS // 2
    d = np.maximum(dist, 1).astype(np.float32)
    large = exact + (np.log(d / np.float32(exact)).astype(np.float32) / np.float32(math.log(MAX_DISTANCE / exact))
                     * np.float32(BUCKETS - exact)).astype(np.int32)
    return np.where(dist < exact, dist, np.minimum(large, BUCKETS - 1))


def _constants():
    dist = SEQ - 1 - np.arange(SPAN)
    bucket = _t5_bucket(np.maximum(dist, 0))
    onehot = (np.arange(BUCKETS)[:, None] == bucket[None, :]).astype(np.float32)
    mult = sum(((dist % d == 0) & (dist <= w)).astype(np.float64) for w, d in BRANCHES)
    row_a = np.where((dist >= 0) & (mult > 0), np.log(np.maximum(mult, 1)), MASKED)
    row_b = np.where(dist >= 0, 0.0, MASKED)
    rowmask = np.stack([row_a] * A_HEADS + [row_b] * B_HEADS).astype(np.float32)
    p, k = np.arange(P)[:, None], np.arange(SEQ)[None, :]
    mask8 = np.where(P + p - k >= 0, 0.0, MASKED / SCALE).astype(np.float32)
    tri = np.stack([(p + P * t <= k) for t in range(TT)], 1).astype(np.float32)
    iota = np.broadcast_to(np.arange(P, dtype=np.float32), (P, P)).copy()
    return {"c_bucket": onehot, "c_rowmask": rowmask, "c_mask8": mask8, "c_tri": tri, "c_iota": iota,
            "c_ident": np.eye(P, dtype=np.float32), "c_flip": np.eye(P, dtype=np.float32)[::-1]}


def _layout(v):
    def rows(w):
        return np.swapaxes(w.reshape(w.shape[:-2] + (KT, P, w.shape[-1])), -3, -2)

    def units(w, starts):
        return np.stack([np.concatenate([rows(w)[:, :, c:c + P] for c in cols], -1) for cols in starts])

    ev, od = v["even_w_in"][0], v["odd_w_in"][0]
    wa = A_HEADS * HEAD
    even = [(P * u, wa + P * u, 2 * wa + P * u) for u in range(4)] + \
           [(3 * wa + P * u, 3 * wa + wa + P * u, 3 * wa + 2 * wa + P * u) for u in range(4)]
    odd = [(P * u, D + P * u, 2 * D + P * u) for u in range(UNITS)]
    wq = v["peer_wq"]
    u = v["peer_u"].reshape(LAYERS, NKEYS, NKEYS, KT, P)
    return {
        "x": v["x"],
        "mix_g": np.swapaxes(v["norm_mix_g"].reshape(LAYERS, KT, P), 1, 2),
        "ffn_g": np.swapaxes(v["norm_ffn_g"].reshape(LAYERS, KT, P), 1, 2),
        "final_g": v["final_norm_g"],
        "rel_bias": v["rel_bias"],
        "diff_lambda": v["diff_lambda"].reshape(-1),
        "diff_ln_g": v["diff_ln_g"].reshape(-1),
        "odd_b_f": v["odd_b_f"].reshape(-1),
        "w_f": rows(od)[:, :, 3 * D:],
        "w_unit": np.stack([units(ev, even), units(od, odd)]),
        "w_out": np.stack([rows(v["even_w_out"][0]), rows(v["odd_w_out"][0])]),
        "w_query": np.transpose(wq.reshape(LAYERS, KT, P, HALVES, P), (0, 3, 2, 1, 4)),
        "subkeys": np.transpose(v["peer_subkeys"].reshape(LAYERS, HALVES, NKEYS, P), (0, 3, 1, 2)),
        "peer_u": np.transpose(u, (0, 2, 4, 3, 1)),
        "peer_v": v["peer_v"].reshape(LAYERS, NKEYS, NKEYS, D),
    }


def kernel(**inputs):
    import concourse.bacc as bacc
    from concourse.bass_utils import run_bass_kernel_spmd

    data = _layout({k: np.asarray(v) for k, v in inputs.items()})
    data.update(_constants())
    nc = bacc.Bacc("TRN2", target_bir_lowering=False, num_devices=1)
    arrays, aps = {}, {}
    for name, arr in data.items():
        arrays["in_" + name] = np.ascontiguousarray(arr)
        aps[name] = nc.dram_tensor("in_" + name, arr.shape, F32, kind="ExternalInput").ap()
    aps["y"] = nc.dram_tensor("out_y", (1, SEQ, D), F32, kind="ExternalOutput").ap()
    build(nc, aps)
    r = run_bass_kernel_spmd(nc, [arrays], core_ids=[0])
    return r.results[0]["out_y"]
```

```python
import math

import numpy as np
import concourse.bass as bass
from concourse import mybir
from contextlib import ExitStack

P = 128
D = 1024
KT = D // P
SEQ = 256
TT = SEQ // P
LAYERS = 2
A_HEADS, B_HEADS, C_HEADS = 8, 4, 16
BIAS_HEADS = A_HEADS + B_HEADS
BUCKETS, MAX_DISTANCE = 32, 2048
BRANCHES = ((128, 1), (512, 4), (2048, 16))
HEAD = 64
SCALE = HEAD ** -0.5
UNITS = D // P
UW = 3 * P
HEADS, TOPK, NKEYS = 8, 16, 128
HALVES = 2 * HEADS
EPS = 1e-6
LAM_INIT = 0.8 - 0.6 * math.exp(-0.3 * 0)
MASKED = -1e30
LOWEST = -3.0e38
SPAN = SEQ + P - 1
TOK_BODY = 16
TOK_HALF = 8

F32 = mybir.dt.float32
F32R = mybir.dt.float32r
U32 = mybir.dt.uint32
ALU = mybir.AluOpType
ACT = mybir.ActivationFunctionType
AX_X = mybir.AxisListType.X


class NormSems:

    def __init__(self, sem):
        self.sq = sem("norm_sumsq")
        self.ms = sem("norm_meansq")
        self.root = sem("norm_root")
        self.hn = sem("norm_scaled")
        self.tr = sem("norm_transposed")
        self.hT = sem("norm_hT")


class ExpertSems:

    def __init__(self, sem):
        self.u_loaded = [sem("u%d_loaded" % b) for b in range(2)]
        self.v_loaded = [sem("v%d_loaded" % b) for b in range(2)]
        self.u_hi = sem("u_hi_ready")
        self.u_split = sem("u_lo_ready")
        self.v_hi = sem("v_hi_ready")
        self.v_split = sem("v_lo_ready")
        self.hT_hi = sem("hT_hi_ready")
        self.hT_split = sem("hT_lo_ready")
        self.seeded = sem("residual_in_accumulators")
        self.act_ready = sem("act_ready")
        self.gelu = sem("gelu_ready")
        self.product = sem("weight_ready")
        self.product_hi = sem("weight_hi_ready")
        self.weighed = sem("weight_lo_ready")
        self.summed = sem("experts_summed")
        self.x_end = sem("x_after_ffn")


class LayerSems:

    def __init__(self, sem, p):
        self.w_loaded = [sem(p + "unit_w%d_loaded" % b) for b in range(2)]
        self.wo_loaded = sem(p + "w_out_loaded")
        self.qk_projected = sem(p + "qk_projected")
        self.v_projected = sem(p + "v_projected")
        self.qk_copied = sem(p + "qk_copied")
        self.v_copied = sem(p + "v_copied")
        self.scores = [sem(p + "scores%d" % m) for m in range(2)]
        self.max_ready = [sem(p + "max%d" % m) for m in range(2)]
        self.probs = [sem(p + "probs%d" % m) for m in range(2)]
        self.pt = [sem(p + "probsT%d" % m) for m in range(2)]
        self.pt_copied = [sem(p + "probsT_copied%d" % m) for m in range(2)]
        self.o_ready = sem(p + "o_ready")
        self.o_normed = sem(p + "o_normed")
        self.unit_step = sem(p + "dve_unit_steps")
        self.ln_ms = sem(p + "diff_ln_ms")
        self.ln_root = sem(p + "diff_ln_root")
        self.ocat = sem(p + "ocat_ready")
        self.o_tr = sem(p + "o_transposed")
        self.oT = sem(p + "oT_ready")
        self.mixed = sem(p + "mixer_out")
        self.x_mid = sem(p + "x_after_mixer")
        self.sk_loaded = sem(p + "subkeys_loaded")
        self.wq_loaded = [sem(p + "wq%d_loaded" % c) for c in range(2)]
        self.q_ready = [sem(p + "q%d" % c) for c in range(2)]
        self.q_copied = [sem(p + "q%d_copied" % c) for c in range(2)]
        self.sc_ready = [sem(p + "sc%d" % c) for c in range(2)]
        self.sc_read = sem(p + "sc_read")
        self.topk_step = sem(p + "dve_topk_steps")
        self.gate_d = sem(p + "gate_logits")
        self.gate_e = sem(p + "gate_exps")
        self.picked = sem(p + "picks_ready")
        self.picks_tr = sem(p + "picks_transposed")
        self.hot = sem(p + "onehots")
        self.gate_mm = sem(p + "gate_products")
        self.gate_copied = [sem(p + "gate_copied%d" % g) for g in range(2)]


def build(nc, a):
    with ExitStack() as ctx:
        def sb(name, shape, dt=F32):
            return ctx.enter_context(nc.sbuf_tensor(name, shape, dt))

        def sem(name):
            return ctx.enter_context(nc.semaphore(name))

        def next_offset():
            return -(-nc.sbuf_base // 32) * 32

        x_at = next_offset()
        x = sb("x", [P, TT, D])
        h_at = next_offset()
        h = sb("h", [P, TT, D])
        hT_at = next_offset()
        hT = sb("hT", [P, KT, SEQ])
        hT_lo = sb("hT_lo", [P, KT, SEQ], F32R)
        region = sb("region", [P, NKEYS * SEQ])
        expert_u = sb("expert_u", [P, 2, KT, P])
        expert_v = sb("expert_v", [P, 2, D])
        u_hi = sb("u_hi", [P, 2, KT, P], F32R)
        u_lo = sb("u_lo", [P, 2, KT, P], F32R)
        onehot1_at = next_offset()
        onehot1 = sb("onehot1", [P, TOK_HALF, P])
        onehot2_at = next_offset()
        onehot2 = sb("onehot2", [P, TOK_HALF, P])
        v_hi = nc.alloc_sbuf_tensor_at("v_hi", [P, 2, D], F32R, offset=x_at)
        v_lo = nc.alloc_sbuf_tensor_at("v_lo", [P, 2, D], F32R, offset=hT_at)
        hT_hi = nc.alloc_sbuf_tensor_at("hT_hi", [P, KT, SEQ], F32R, offset=h_at)
        gelu_act = nc.alloc_sbuf_tensor_at("gelu_act", [P, 2, SEQ], F32, offset=onehot1_at)
        weight = nc.alloc_sbuf_tensor_at("weight", [P, 2, SEQ], F32, offset=onehot1_at + 2 * SEQ * 4)
        weight_hi = nc.alloc_sbuf_tensor_at("weight_hi", [P, 2, SEQ], F32R, offset=onehot2_at)
        weight_lo = nc.alloc_sbuf_tensor_at("weight_lo", [P, 2, SEQ], F32R, offset=onehot2_at + 2 * SEQ * 4)
        picksT = sb("picksT", [P, 3, SEQ])
        ident = sb("ident", [P, P])
        iota = sb("iota", [P, P])
        gains = sb("gains", [P, 2 * LAYERS, KT])
        sumsq = sb("sumsq", [P, TT])
        rstd = sb("rstd", [P, TT])
        lam_in = sb("lam_in", [P, 4 * HEAD])
        lam = sb("lam", [P, 4])
        neg_max = sb("neg_max", [P, 2, TT])
        denom = sb("denom", [P, 2, TT])
        rdenom = sb("rdenom", [P, 2, TT])
        ln_ss = sb("ln_ss", [P, TT * B_HEADS])
        b_f = sb("b_f", [P, C_HEADS])
        w_f = sb("w_f", [P, KT, C_HEADS])
        logsig = sb("logsig", [P, TT, C_HEADS])
        lse_tmp = sb("lse_tmp", [P, TT, C_HEADS])
        cum8 = sb("cum8", [P, TT, C_HEADS])
        ps = ctx.enter_context(nc.psum_tensor("ps", [P, 8, 512], F32))

        gate = region[:, :].rearrange("p (i t) -> p i t", i=NKEYS)
        at = [0]

        def carve(shape, like=None):
            n = int(np.prod(shape))
            v = region[:, at[0]:at[0] + n]
            at[0] += n
            assert at[0] <= NKEYS * SEQ
            if len(shape) == 1:
                return v
            names = "abcdef"[:len(shape)]
            return v.rearrange("p (%s) -> p %s" % (" ".join(names), " ".join(names)),
                               **{c: s for c, s in zip(names, shape)})

        bias8 = carve([BIAS_HEADS, SEQ])
        cumT8 = carve([C_HEADS, SEQ])
        mask8 = carve([SEQ])
        w_unit = carve([2, KT, UW])
        w_out = carve([KT, D])
        qkT = carve([2, 512])
        val = carve([2, TT, P])
        logits = carve([2, 384])
        probs = carve([2, 384])
        probsT = carve([2, 384])
        map_bias = carve([2, 384])
        tri = carve([TT, SEQ])
        ln_g = carve([P])
        row_in = carve([SPAN + 1])
        row_mask = carve([SPAN + 1])
        row_out = carve([SPAN + 1])
        cumT_row = carve([SEQ])
        o_sq = carve([TT * B_HEADS, P])
        flip = carve([P])
        hankel = carve([BIAS_HEADS, SEQ])
        at[0] = 0
        subkeys = carve([HALVES, P])
        qTs = carve([2, SEQ])
        left = carve([2, TT, P])
        cand = carve([TT, TOPK, TOPK])
        cand_left = carve([TT, TOPK, TOPK])
        head_v = carve([TT, 2, TOPK])
        head_i = carve([TT, 2, TOPK]).bitcast(U32)
        head_best = carve([TT, TOPK])
        head_j = carve([TT, TOPK]).bitcast(U32)
        top_if = carve([TT, HEADS, 2, TOPK])
        best_v = carve([TT, HEADS, TOPK])
        best_j = carve([TT, HEADS, TOPK]).bitcast(U32)
        slot_i = carve([TT * HEADS, TOPK]).bitcast(U32)
        slot_f = carve([2, TT * HEADS, TOPK])
        hit = carve([TT * HEADS, TOPK, TOPK])
        gate_z = carve([TT * HEADS])
        picks = carve([3, TT, P])

        s_const = sem("const_loaded")
        s_row = sem("row_inputs_loaded")
        s_x = sem("x_loaded")
        s_scratch = sem("bias_row_stored")
        s_bias = sem("bias_tiles_loaded")
        s_flip = sem("bias_tiles_flipped")
        s_flipped = sem("bias_tiles_ready")
        s_rowmm = sem("bias_row_product")
        s_rowdone = sem("bias_row_done")
        s_lamsum = sem("lambda_sums")
        s_lamexp = sem("lambda_exps")
        dve_straight = sem("dve_straight_steps")
        waited = sem("dve_waited_in_a_loop")
        act_straight = sem("act_straight_steps")
        s_fgw = sem("forget_weights_loaded")
        s_fg = sem("forget_logits")
        s_fgneg = sem("forget_neg_abs")
        s_fgln = sem("forget_ln")
        s_fglog = sem("forget_logsigmoid")
        s_cum = sem("forget_cumsum")
        s_cumrow = sem("forget_row_done")
        s_cumst = sem("forget_row_stored")
        s_cumld = sem("forget_tiles_loaded")
        s_fgain = sem("final_gain_loaded")
        s_y = sem("output_ready")
        s_out = sem("output_stored")

        MIX, FFN, LAST = [0, 2], [1, 3], 2 * LAYERS
        norms = NormSems(sem)
        ex = ExpertSems(sem)
        L = [LayerSems(sem, "L%d_" % n) for n in range(LAYERS)]

        bias_row = nc.dram_tensor("bias_row", (BIAS_HEADS, SPAN), F32, kind="Internal").ap()
        cum_row = nc.dram_tensor("cum_row", (C_HEADS, SEQ), F32, kind="Internal").ap()
        bias_src = bass.AP(tensor=bias_row.tensor, offset=0, ap=[[1, P], [SPAN, BIAS_HEADS], [1, SEQ]])
        FLIP_BANKS = (0, 1, 2, 3, 6, 7)

        def free(u):
            return u + 1

        def done(u):
            return u + 2

        def credit(eng, *sems):
            for x in sems:
                eng.sem_inc(x, 1)

        def over_pairs(eng, n, body, straight=False):
            if n == 0:
                with eng.Fori(0, 2) as i:
                    body("A", i, False)
                body("B", 2, False)
                body("B", 3, True)
            else:
                with eng.Fori(0, 3) as i:
                    body("C", i, False)
                body("C", 3, True)

        block = ctx.enter_context(nc.Block())

        @block.sync
        def _(sp):
            sp.dma_start(x[:, :, :], a["x"].rearrange("b (tt p) d -> p (b tt) d", p=P)).then_inc(s_x, 16)
            sp.dma_start(row_in[0:BUCKETS, 0:SPAN], a["c_bucket"]).then_inc(s_row, 16)
            sp.dma_start(row_out[0:BUCKETS, 0:BIAS_HEADS], a["rel_bias"]).then_inc(s_row, 16)
            sp.dma_start(row_mask[0:BIAS_HEADS, 0:SPAN], a["c_rowmask"]).then_inc(s_row, 16)
            sp.dma_start(ident[:, :], a["c_ident"]).then_inc(s_const, 16)
            sp.dma_start(iota[:, :], a["c_iota"]).then_inc(s_const, 16)
            sp.dma_start(flip, a["c_flip"]).then_inc(s_const, 16)
            for n in range(LAYERS):
                sp.dma_start(gains[:, 2 * n, :], a["mix_g"][n]).then_inc(s_const, 16)
                sp.dma_start(gains[:, 2 * n + 1, :], a["ffn_g"][n]).then_inc(s_const, 16)
            sp.dma_start(lam_in[:, :], a["diff_lambda"].partition_broadcast(P)).then_inc(s_const, 16)
            sp.dma_start(ln_g, a["diff_ln_g"].partition_broadcast(P)).then_inc(s_const, 16)
            sp.dma_start(b_f[:, :], a["odd_b_f"].partition_broadcast(P)).then_inc(s_const, 16)
            sp.dma_start(w_f[:, :, :], a["w_f"]).then_inc(s_const, 16)
            for n in range(LAYERS):
                s = L[n]
                if n > 0:
                    sp.wait_ge(ex.product, n * NKEYS)
                    sp.dma_start(tri, a["c_tri"]).then_inc(s_fgw, 16)
                    sp.dma_start(mask8, a["c_mask8"]).then_inc(s_fgw, 16)
                for b in range(2):
                    sp.dma_start(w_unit[:, b], a["w_unit"][n, b]).then_inc(s.w_loaded[b], 16)
                sp.dma_start(w_out, a["w_out"][n]).then_inc(s.wo_loaded, 16)
                if n == 0:
                    sp.wait_ge(s_rowdone, 1)
                    sp.dma_start(bias_row, row_out[0:BIAS_HEADS, 0:SPAN]).then_inc(s_scratch, 16)
                    sp.wait_ge(s_scratch, 16)
                    sp.dma_start(hankel, bias_src).then_inc(s_bias, 16)
                else:
                    sp.wait_ge(s_cumrow, 1)
                    sp.dma_start(cum_row, cumT_row[0:C_HEADS, :]).then_inc(s_cumst, 16)
                    sp.wait_ge(s_cumst, 16)
                    sp.dma_start(cumT8, cum_row.rearrange("h t -> (h t)").partition_broadcast(P)
                                 .rearrange("p (h t) -> p h t", h=C_HEADS)).then_inc(s_cumld, 16)
                with sp.Fori(1, UNITS // 2) as i:
                    for b in range(2):
                        sp.wait_ge(s.v_projected, 2 * i + b - 1)
                        sp.dma_start(w_unit[:, b], a["w_unit"][n, 2 * i + b]).then_inc(s.w_loaded[b], 16)
                for c in range(2):
                    sp.dma_start(expert_u[:, c], a["w_query"][n, c]).then_inc(s.wq_loaded[c], 16)
                sp.wait_ge(s.mixed, 1)
                sp.wait_ge(s.x_mid, 2)
                sp.dma_start(subkeys, a["subkeys"][n]).then_inc(s.sk_loaded, 16)
                with sp.Fori(1, HEADS) as i:
                    for c in range(2):
                        sp.wait_ge(s.q_ready[c], i)
                        sp.dma_start(expert_u[:, c], a["w_query"][n, 2 * i + c]).then_inc(s.wq_loaded[c], 16)
                for b in range(2):
                    sp.wait_ge(s.q_ready[b], HEADS)
                    sp.dma_start(expert_u[:, b], a["peer_u"][n, b]).then_inc(ex.u_loaded[b], 16)
                    sp.dma_start(expert_v[:, b, :], a["peer_v"][n][:, b, :]).then_inc(ex.v_loaded[b], 16)
                with sp.Fori(1, NKEYS // 2) as i:
                    for b in range(2):
                        last_c = n * NKEYS + 2 * (i - 1) + b
                        sp.wait_ge(ex.u_split, last_c + 1)
                        sp.dma_start(expert_u[:, b], a["peer_u"][n, 2 * i + b]).then_inc(ex.u_loaded[b], 16)
                        sp.wait_ge(ex.v_split, last_c + 1)
                        sp.dma_start(expert_v[:, b, :], a["peer_v"][n][:, 2 * i + b, :]).then_inc(ex.v_loaded[b], 16)
            sp.wait_ge(ex.v_split, LAYERS * NKEYS)
            sp.dma_start(expert_v[:, 0, :], a["final_g"].partition_broadcast(P)).then_inc(s_fgain, 16)
            sp.wait_ge(s_y, 1)
            sp.dma_start(a["y"].rearrange("b (tt p) d -> p (b tt) d", p=P), h[:, :, :]).then_inc(s_out, 16)
            sp.wait_ge(s_out, 16)

        @block.tensor
        def _(pe):
            def turn(ready, ready_at, done):
                pe.wait_ge(ready, ready_at)
                for kt in range(KT):
                    for tt in range(TT):
                        c = (kt % 2) * SEQ + tt * P
                        last = pe.transpose(ps[:, kt // 2, c:c + P], h[:, tt, kt * P:(kt + 1) * P], ident[:, :])
                    if kt % 2:
                        last.then_inc(done, 1)

            def project_unit(s, b, u, i):
                pe.wait_ge(s.w_loaded[b], 16 * (i + 1))
                pe.wait_ge(s.qk_copied, free(u))
                for part in range(2):
                    for kt in range(KT):
                        last = pe.matmul(ps[:, 4, part * SEQ:(part + 1) * SEQ],
                                         w_unit[:, b, kt, part * P:(part + 1) * P], hT[:, kt, :],
                                         start=(kt == 0), stop=(kt == KT - 1))
                last.then_inc(s.qk_projected, 1)
                pe.wait_ge(s.v_copied, free(u))
                for tt in range(TT):
                    for kt in range(KT):
                        last = pe.matmul(ps[:, 5, tt * P:(tt + 1) * P], hT[:, kt, tt * P:(tt + 1) * P],
                                         w_unit[:, b, kt, 2 * P:3 * P], start=(kt == 0), stop=(kt == KT - 1))
                last.then_inc(s.v_projected, 1)

            def attend(s, kind, b, u):
                pe.wait_ge(s.qk_copied, done(u))
                for m in range(2):
                    r = slice(m * HEAD, (m + 1) * HEAD)
                    pe.wait_ge(s.pt_copied[m], free(u))
                    pe.matmul(ps[:, 6 + m, 0:P], qkT[r, b, 0:P], qkT[r, b, SEQ:SEQ + P], start=True, stop=True)
                    pe.matmul(ps[:, 6 + m, P:3 * P], qkT[r, b, P:SEQ], qkT[r, b, SEQ:2 * SEQ],
                              start=True, stop=True).then_inc(s.scores[m], 1)

            def combine(s, kind, b, u):
                for m in range(2):
                    pe.wait_ge(s.probs[m], done(u))
                    for blk in range(3):
                        last = pe.transpose(ps[:, 6 + m, blk * P:(blk + 1) * P],
                                            probs[:, m, blk * P:(blk + 1) * P], ident[:, :])
                    last.then_inc(s.pt[m], 1)
                pe.wait_ge(s.v_copied, done(u))
                pe.wait_ge(s.o_normed, free(u))
                w = P if kind == "B" else HEAD
                for m in range(2):
                    pe.wait_ge(s.pt_copied[m], done(u))
                    v0 = 0 if kind == "B" else m * HEAD
                    out = [ps[:, 0, (tt * 2 + m) * w:(tt * 2 + m + 1) * w] for tt in range(TT)]
                    pe.matmul(out[0], probsT[:, m, 0:P], val[:, b, 0, v0:v0 + w], start=True, stop=True)
                    pe.matmul(out[1], probsT[:, m, P:2 * P], val[:, b, 0, v0:v0 + w], start=True, stop=False)
                    last = pe.matmul(out[1], probsT[:, m, 2 * P:3 * P], val[:, b, 1, v0:v0 + w],
                                     start=False, stop=True)
                last.then_inc(s.o_ready, 1)

            for s in L:
                credit(pe, *s.pt, *s.sc_ready)

            pe.wait_ge(s_row, 48)
            pe.matmul(ps[0:BIAS_HEADS, 5, 0:SPAN], row_out[0:BUCKETS, 0:BIAS_HEADS], row_in[0:BUCKETS, 0:SPAN],
                      start=True, stop=True).then_inc(s_rowmm, 1)
            pe.wait_ge(s_const, 16 * (7 + 2 * LAYERS))
            for n in range(LAYERS):
                s = L[n]
                turn(norms.hn, TT * (MIX[n] + 1), norms.tr)
                pe.wait_ge(norms.hT, KT * (MIX[n] + 1))
                if n == 0:
                    pe.wait_ge(s_rowdone, 1)
                if n == 1:
                    for tt in range(TT):
                        for kt in range(KT):
                            last = pe.matmul(ps[:, 2, tt * C_HEADS:(tt + 1) * C_HEADS],
                                             hT[:, kt, tt * P:(tt + 1) * P], w_f[:, kt, :],
                                             start=(kt == 0), stop=(kt == KT - 1))
                    last.then_inc(s_fg, 1)
                project_unit(s, 0, 0, 0)
                if n == 0:
                    pe.wait_ge(s_bias, 16)
                    for j, bank in enumerate(FLIP_BANKS):
                        last = pe.matmul(ps[:, bank, :], flip,
                                         hankel[:, 2 * j:2 * j + 2, :].rearrange("p h k -> p (h k)"),
                                         start=True, stop=True)
                    last.then_inc(s_flip, 1)
                    pe.wait_ge(s_flipped, len(FLIP_BANKS))
                if n == 1:
                    pe.wait_ge(s_fglog, 1)
                    pe.wait_ge(s_fgw, 32)
                    for tt in range(TT):
                        for kt in range(TT):
                            pe.matmul(ps[:, 2, tt * C_HEADS:(tt + 1) * C_HEADS], tri[:, kt, tt * P:(tt + 1) * P],
                                      logsig[:, kt, :], start=(kt == 0), stop=(kt == TT - 1))
                    for kt in range(TT):
                        last = pe.matmul(ps[0:C_HEADS, 3, 0:SEQ], logsig[:, kt, :], tri[:, kt, :],
                                         start=(kt == 0), stop=(kt == TT - 1))
                    last.then_inc(s_cum, 1)

                def pair(kind, i, last_pair):
                    for b in range(2):
                        u = 2 * i + b
                        attend(s, kind, b, u)
                        if not (last_pair and b):
                            project_unit(s, 1 - b, u + 1, i + b)
                        combine(s, kind, b, u)

                over_pairs(pe, n, pair)

                turn(*((s.ocat, 1) if n == 0 else (s.o_normed, free(UNITS))), s.o_tr)
                pe.wait_ge(s.oT, KT)
                pe.wait_ge(s.wo_loaded, 16)
                for tt in range(TT):
                    for half in range(2):
                        for kt in range(KT):
                            last = pe.matmul(ps[:, 4 + 2 * tt + half, :], hT[:, kt, tt * P:(tt + 1) * P],
                                             w_out[:, kt, half * 512:(half + 1) * 512],
                                             start=(kt == 0), stop=(kt == KT - 1))
                    last.then_inc(s.mixed, 1)

                turn(norms.hn, TT * (FFN[n] + 1), norms.tr)
                pe.wait_ge(norms.hT, KT * (FFN[n] + 1))
                pe.wait_ge(s.sk_loaded, 16)
                with pe.Fori(0, HEADS) as i:
                    for c in range(2):
                        pe.wait_ge(s.wq_loaded[c], 16 * (i + 1))
                        pe.wait_ge(s.q_copied[c], free(i))
                        for kt in range(KT):
                            last = pe.matmul(ps[:, 4 + c, 0:SEQ], expert_u[:, c, kt, :], hT[:, kt, :],
                                             start=(kt == 0), stop=(kt == KT - 1))
                        last.then_inc(s.q_ready[c], 1)
                    for c in range(2):
                        pe.wait_ge(s.q_copied[c], done(i))
                        if c == 0:
                            pe.wait_ge(s.sc_read, free(i))
                        for tt in range(TT):
                            last = pe.matmul(ps[:, 6 + c, tt * P:(tt + 1) * P], qTs[:, c, tt * P:(tt + 1) * P],
                                             subkeys[:, 2 * i + c, :], start=True, stop=True)
                        last.then_inc(s.sc_ready[c], 1)

                for tt in range(TT):
                    for half in range(2):
                        last = pe.matmul(ps[:, 2 * tt + half, :], ident[:, :], x[:, tt, half * 512:(half + 1) * 512],
                                         start=True, stop=False)
                last.then_inc(ex.seeded, 1)

                pe.wait_ge(s.picked, 1)
                for w in range(3):
                    for tt in range(TT):
                        c = w * SEQ + tt * P
                        last = pe.transpose(ps[:, 4 + c // 512, c % 512:c % 512 + P], picks[:, w, tt, :], ident[:, :])
                last.then_inc(s.picks_tr, 1)

                with pe.Fori(0, SEQ // TOK_BODY) as i:
                    for g in range(2):
                        pe.wait_ge(s.gate_copied[g], free(i))
                        for j in range(TOK_HALF):
                            pe.wait_ge(s.hot, TOK_BODY * i + TOK_HALF * g + j + 1)
                            pe.matmul(ps[:, 4 + 2 * g + j // 4, (j % 4) * P:(j % 4 + 1) * P], onehot1[:, j, :],
                                      onehot2[:, j, :], start=True, stop=True).then_inc(s.gate_mm, 1)

                pe.wait_ge(s.gate_copied[0], free(SEQ // TOK_BODY))
                pe.wait_ge(ex.hT_split, n + 1)
                first = n * NKEYS

                def experts_in(b, c):
                    pe.wait_ge(ex.u_split, c + 1)
                    for kt in range(KT):
                        for w, t in ((u_hi, hT_hi), (u_hi, hT_lo), (u_lo, hT_hi)):
                            last = pe.matmul(ps[:, 4 + b, 0:SEQ], w[:, b, kt, :], t[:, kt, :],
                                             start=(kt == 0 and w is u_hi and t is hT_hi),
                                             stop=(kt == KT - 1 and w is u_lo))
                    last.then_inc(ex.act_ready, 1)

                def experts_out(b, c, stop):
                    pe.wait_ge(ex.v_split, c + 1)
                    pe.wait_ge(ex.weighed, c + 1)
                    for tt in range(TT):
                        for w, v in ((weight_hi, v_hi), (weight_hi, v_lo), (weight_lo, v_hi)):
                            for half in range(2):
                                last = pe.matmul(ps[:, 2 * tt + half, :], w[:, b, tt * P:(tt + 1) * P],
                                                 v[:, b, half * 512:(half + 1) * 512], start=False,
                                                 stop=(stop and w is weight_lo))
                    last.then_inc(ex.summed, 1)

                experts_in(0, first)
                with pe.Fori(0, NKEYS // 2 - 1) as i:
                    c = first + 2 * i
                    experts_in(1, c + 1)
                    experts_out(0, c, False)
                    experts_in(0, c + 2)
                    experts_out(1, c + 1, False)
                c = first + NKEYS - 2
                experts_in(1, c + 1)
                experts_out(0, c, False)
                experts_out(1, c + 1, True)

        @block.scalar
        def _(act):
            for s in L:
                credit(act, s.qk_copied, s.v_copied, *s.probs, *s.q_copied, *s.gate_copied)

            def norm(k, ready, ready_at):
                act.wait_ge(ready, ready_at)
                for tt in range(TT):
                    act.activation(h[:, tt, :], x[:, tt, :], ACT.Square, accum_out=sumsq[:, tt:tt + 1]).then_inc(norms.sq, 1)
                act.wait_ge(norms.ms, k + 1)
                act.activation(rstd[:, :], sumsq[:, :], ACT.Sqrt).then_inc(norms.root, 1)

            for n in range(LAYERS):
                s = L[n]
                if n == 0:
                    norm(MIX[0], s_x, 16)
                    act.wait_ge(s_lamsum, 1)
                    act.activation(lam[:, 2:4], lam[:, 0:2], ACT.Exp).then_inc(s_lamexp, 1)
                else:
                    norm(MIX[n], ex.x_end, 2 * n)
                    act.wait_ge(s_fgneg, 1)
                    act.activation(lse_tmp[:, :, :], lse_tmp[:, :, :], ACT.Exp).then_inc(act_straight, 1)
                    act.wait_ge(s_fgneg, 2)
                    act.activation(lse_tmp[:, :, :], lse_tmp[:, :, :], ACT.Ln).then_inc(s_fgln, 1)

                def copy_unit(b, u):
                    act.wait_ge(s.qk_projected, u + 1)
                    act.copy(qkT[:, b, :], ps[:, 4, :]).then_inc(s.qk_copied, 1)
                    act.wait_ge(s.v_projected, u + 1)
                    act.copy(val[:, b, :, :], ps[:, 5, 0:TT * P].rearrange("p (t c) -> p t c", t=TT))\
                       .then_inc(s.v_copied, 1)

                def pair(kind, i, last_pair):
                    for b in range(2):
                        u = 2 * i + b
                        for m in range(2):
                            act.wait_ge(s.max_ready[m], u + 1)
                            act.wait_ge(s.pt[m], free(u))
                            act.wait_ge(s.o_normed, free(u))
                            act.activation(probs[:, m, 0:P], logits[:, m, 0:P], ACT.Exp,
                                           bias=neg_max[:, m, 0:1], scale=-1.0, accum_out=denom[:, m, 0:1])
                            act.activation(probs[:, m, P:3 * P], logits[:, m, P:3 * P], ACT.Exp,
                                           bias=neg_max[:, m, 1:2], scale=-1.0, accum_out=denom[:, m, 1:2])\
                               .then_inc(s.probs[m], 1)
                        if not (last_pair and b):
                            copy_unit(1 - b, u + 1)

                copy_unit(0, 0)
                over_pairs(act, n, pair)
                if n == 0:
                    act.wait_ge(s.ln_ms, 1)
                    act.activation(ln_ss[:, :], ln_ss[:, :], ACT.Sqrt).then_inc(s.ln_root, 1)
                norm(FFN[n], s.x_mid, 2)

                act.wait_ge(norms.hT, KT * (FFN[n] + 1))
                act.copy(hT_hi[:, :, :], hT[:, :, :]).then_inc(ex.hT_hi, 1)

                with act.Fori(0, HEADS) as i:
                    for c in range(2):
                        act.wait_ge(s.q_ready[c], i + 1)
                        act.wait_ge(s.sc_ready[c], free(i))
                        act.copy(qTs[:, c, :], ps[:, 4 + c, 0:SEQ]).then_inc(s.q_copied[c], 1)
                act.wait_ge(s.gate_d, 1)
                act.activation(best_v, best_v, ACT.Exp).then_inc(s.gate_e, 1)

                def round_u(b, c, turn):
                    act.wait_ge(ex.u_loaded[b], 16 * (turn + 1))
                    act.copy(u_hi[:, b], expert_u[:, b]).then_inc(ex.u_hi, 1)

                def round_v(b, c, turn):
                    act.wait_ge(ex.v_loaded[b], 16 * (turn + 1))
                    act.copy(v_hi[:, b, :], expert_v[:, b, :]).then_inc(ex.v_hi, 1)

                first, turn0 = n * NKEYS, n * NKEYS // 2
                round_u(0, first, turn0)
                round_u(1, first + 1, turn0)
                act.wait_ge(ex.seeded, n + 1)
                round_v(0, first, turn0)

                act.wait_ge(s.hot, 1)
                with act.Fori(0, SEQ // TOK_BODY) as i:
                    for g in range(2):
                        act.wait_ge(s.gate_mm, TOK_BODY * i + TOK_HALF * (g + 1))
                        act.copy(gate[:, :, bass.ds(TOK_BODY * i + TOK_HALF * g, TOK_HALF)],
                                 ps[:, 4 + 2 * g:6 + 2 * g, :].rearrange("p b (t i) -> p i (b t)", t=4))\
                           .then_inc(s.gate_copied[g], 1)

                def activate(b, c):
                    act.wait_ge(ex.act_ready, c + 1)
                    act.activation(gelu_act[:, b, :], ps[:, 4 + b, 0:SEQ], ACT.Gelu).then_inc(ex.gelu, 1)

                activate(0, first)
                round_u(0, first + 2, turn0 + 1)
                round_v(1, first + 1, turn0)
                with act.Fori(0, NKEYS // 2 - 2) as i:
                    c = first + 2 * i + 1
                    for b in (1, 0):
                        activate(b, c)
                        round_u(b, c + 2, turn0 + i + 1 + (1 - b))
                        act.wait_ge(ex.summed, c)
                        round_v(1 - b, c + 1, turn0 + i + 1)
                        c = c + 1
                c = first + NKEYS - 3
                activate(1, c)
                round_u(1, c + 2, turn0 + NKEYS // 2 - 1)
                act.wait_ge(ex.summed, c)
                round_v(0, c + 1, turn0 + NKEYS // 2 - 1)
                activate(0, c + 1)
                act.wait_ge(ex.summed, c + 1)
                round_v(1, c + 2, turn0 + NKEYS // 2 - 1)
                activate(1, c + 2)
                act.wait_ge(ex.summed, first + NKEYS)
                for half in range(2):
                    last = act.copy(x[:, 1, half * 512:(half + 1) * 512], ps[:, 2 + half, :])
                last.then_inc(ex.x_end, 1)
            norm(LAST, ex.x_end, 2 * LAYERS)

        @block.vector
        def _(dve):
            straight = [0]

            def then(ins):
                straight[0] += 1
                ins.then_inc(dve_straight, 1)
                dve.wait_ge(dve_straight, straight[0])

            def wait_apart(sem, value):
                dve.wait_ge(sem, value)
                dve.sem_inc(waited, 1)

            class Steps:

                def __init__(self, sem, turns, per):
                    self.sem, self.base, self.n = sem, turns * per, 0

                def add(self, ins):
                    self.n += 1
                    ins.then_inc(self.sem, 1)
                    return self.n

                def wait(self, k):
                    wait_apart(self.sem, self.base + k)

            def norm_scale(k):
                dve.wait_ge(norms.sq, TT * (k + 1))
                dve.tensor_scalar(sumsq[:, :], sumsq[:, :], 1.0 / D, EPS, ALU.mult, ALU.add).then_inc(norms.ms, 1)
                dve.wait_ge(norms.root, k + 1)
                then(dve.reciprocal(rstd[:, :], rstd[:, :]))

            def norm(k):
                norm_scale(k)
                for tt in range(TT):
                    dve.tensor_scalar(h[:, tt, :], x[:, tt, :], rstd[:, tt:tt + 1], None, ALU.mult).then_inc(norms.hn, 1)
                for kt in range(KT):
                    if kt % 2 == 0:
                        dve.wait_ge(norms.tr, KT // 2 * k + kt // 2 + 1)
                    dve.tensor_scalar(hT[:, kt, :], ps[:, kt // 2, (kt % 2) * SEQ:(kt % 2 + 1) * SEQ],
                                      gains[:, k, kt:kt + 1], None, ALU.mult).then_inc(norms.hT, 1)

            for s in L:
                credit(dve, *s.pt_copied, s.o_normed, s.sc_read)

            dve.wait_ge(s_rowmm, 1)
            then(dve.tensor_tensor(row_mask[0:BIAS_HEADS, 0:SPAN], ps[0:BIAS_HEADS, 5, 0:SPAN],
                                   row_mask[0:BIAS_HEADS, 0:SPAN], ALU.add))
            dve.tensor_scalar(row_out[0:BIAS_HEADS, 0:SPAN], row_mask[0:BIAS_HEADS, 0:SPAN], 1.0 / SCALE, None,
                              ALU.mult).then_inc(s_rowdone, 1)
            dve.wait_ge(s_const, 16 * (7 + 2 * LAYERS))
            for j in range(2):
                last = dve.tensor_tensor_reduce(lam_in[:, 2 * j * HEAD:(2 * j + 1) * HEAD],
                                                lam_in[:, 2 * j * HEAD:(2 * j + 1) * HEAD],
                                                lam_in[:, (2 * j + 1) * HEAD:(2 * j + 2) * HEAD], 1.0, 0.0,
                                                ALU.mult, ALU.add, lam[:, j:j + 1])
            last.then_inc(s_lamsum, 1)

            for n in range(LAYERS):
                s = L[n]
                norm(MIX[n])
                if n == 0:
                    dve.wait_ge(s_lamexp, 1)
                    then(dve.tensor_tensor(lam[:, 0:1], lam[:, 3:4], lam[:, 2:3], ALU.subtract))
                    then(dve.tensor_scalar(lam[:, 0:1], lam[:, 0:1], -LAM_INIT, None, ALU.add))
                    then(dve.tensor_scalar(ln_g, ln_g, 1.0 - LAM_INIT, None, ALU.mult))
                    dve.wait_ge(s_flip, 1)
                    for j, bank in enumerate(FLIP_BANKS):
                        dve.tensor_copy(bias8[:, 2 * j:2 * j + 2, :],
                                        ps[:, bank, :].rearrange("p (h k) -> p h k", h=2)).then_inc(s_flipped, 1)
                    dve.wait_ge(s_flipped, len(FLIP_BANKS))
                else:
                    dve.wait_ge(s_fg, 1)
                    fg = ps[:, 2, 0:TT * C_HEADS].rearrange("p (t h) -> p t h", t=TT)
                    for tt in range(TT):
                        ins = dve.tensor_tensor(logsig[:, tt, :], fg[:, tt, :], b_f[:, :], ALU.add)
                    then(ins)
                    dve.scalar_tensor_tensor(lse_tmp[:, :, :], logsig[:, :, :], -1.0, logsig[:, :, :], ALU.mult, ALU.min)\
                       .then_inc(s_fgneg, 1)
                    then(dve.tensor_scalar(logsig[:, :, :], logsig[:, :, :], 0.0, None, ALU.min))
                    dve.wait_ge(act_straight, 1)
                    dve.tensor_scalar(lse_tmp[:, :, :], lse_tmp[:, :, :], 1.0, None, ALU.add).then_inc(s_fgneg, 1)
                    dve.wait_ge(s_fgln, 1)
                    dve.tensor_tensor(logsig[:, :, :], logsig[:, :, :], lse_tmp[:, :, :], ALU.subtract)\
                       .then_inc(s_fglog, 1)
                    dve.wait_ge(s_cum, 1)
                    dve.tensor_scalar(cumT_row[0:C_HEADS, :], ps[0:C_HEADS, 3, 0:SEQ], -1.0 / SCALE, None,
                                      ALU.mult).then_inc(s_cumrow, 1)
                    then(dve.tensor_scalar(cum8[:, :, :], fg, 1.0 / SCALE, None, ALU.mult))
                    dve.wait_ge(s_fgw, 32)
                    dve.wait_ge(s_cumld, 16)

                steps_per_unit = {"A": 3, "B": 5, "C": 3}

                def pair(kind, i, last_pair):
                    st = Steps(s.unit_step, i if kind != "B" else i, 2 * steps_per_unit[kind])
                    if kind == "B":
                        st.base = 4 * steps_per_unit["A"] + (i - 2) * 2 * steps_per_unit["B"]
                    for b in range(2):
                        u = 2 * i + b
                        for m in range(2):
                            if kind == "C":
                                hd = 2 * u + m
                                dve.scalar_tensor_tensor(map_bias[:, m, 0:P], cumT8[:, hd, 0:P], cum8[:, 0, bass.ds(hd, 1)],
                                                         mask8[:, P:SEQ], ALU.add, ALU.add)
                                k = st.add(dve.scalar_tensor_tensor(map_bias[:, m, P:3 * P], cumT8[:, hd, :],
                                                                    cum8[:, 1, bass.ds(hd, 1)],
                                                                    mask8, ALU.add, ALU.add))
                                t0 = map_bias[:, m, 0:P]
                            else:
                                hd = 2 * u + m if kind == "A" else A_HEADS + u - A_HEADS // 2
                                k = st.add(dve.tensor_copy(map_bias[:, m, P:3 * P], bias8[:, hd, :]))
                                t0 = map_bias[:, m, 2 * P:3 * P]
                            t1 = map_bias[:, m, P:3 * P]
                            st.wait(k)
                            dve.wait_ge(s.scores[m], u + 1)
                            wait_apart(s.probs[m], free(u))
                            dve.tensor_tensor_reduce(logits[:, m, 0:P], ps[:, 6 + m, 0:P], t0, -SCALE, -LOWEST,
                                                     ALU.add, ALU.min, neg_max[:, m, 0:1])
                            dve.tensor_tensor_reduce(logits[:, m, P:3 * P], ps[:, 6 + m, P:3 * P], t1, -SCALE,
                                                     -LOWEST, ALU.add, ALU.min, neg_max[:, m, 1:2])\
                               .then_inc(s.max_ready[m], 1)
                        for m in range(2):
                            dve.wait_ge(s.pt[m], done(u))
                            dve.tensor_copy(probsT[:, m, :], ps[:, 6 + m, 0:3 * P]).then_inc(s.pt_copied[m], 1)
                        k = st.add(dve.reciprocal(rdenom[:, :, :], denom[:, :, :]))
                        st.wait(k)
                        dve.wait_ge(s.o_ready, u + 1)
                        if kind == "B":
                            k = st.add(dve.tensor_scalar(rdenom[:, 1, :], rdenom[:, 1, :], lam[:, 0:1], None, ALU.mult))
                            st.wait(k)
                            hu = h[:, :, :].rearrange("p t (u c) -> p t u c", u=UNITS)[:, :, u, :]
                            for tt in range(TT):
                                ins = dve.tensor_scalar(hu[:, tt, :], ps[:, 0, tt * 2 * P:(tt * 2 + 1) * P],
                                                        rdenom[:, 0, tt:tt + 1], None, ALU.mult)
                            k = st.add(ins)
                            st.wait(k)
                            for tt in range(TT):
                                ins = dve.scalar_tensor_tensor(hu[:, tt, :], ps[:, 0, (tt * 2 + 1) * P:(tt * 2 + 2) * P],
                                                               rdenom[:, 1, tt:tt + 1], hu[:, tt, :], ALU.mult, ALU.add)
                        else:
                            hu = h[:, :, :].rearrange("p t (u m c) -> p t u m c", u=UNITS, m=2)
                            for m in range(2):
                                for tt in range(TT):
                                    ins = dve.tensor_scalar(hu[:, tt, u, m, :],
                                                            ps[:, 0, (tt * 2 + m) * HEAD:(tt * 2 + m + 1) * HEAD],
                                                            rdenom[:, m, tt:tt + 1], None, ALU.mult)
                        ins.then_inc(s.o_normed, 1)
                    assert st.n == 2 * steps_per_unit[kind]

                over_pairs(dve, n, pair)
                if n == 0:
                    dve.wait_ge(s.o_normed, free(UNITS))
                    ob = h[:, :, :].rearrange("p t (u c) -> p t u c", u=UNITS)
                    for tt in range(TT):
                        for b in range(B_HEADS):
                            j = tt * B_HEADS + b
                            ins = dve.tensor_tensor_reduce(o_sq[:, j, :], ob[:, tt, 4 + b, :], ob[:, tt, 4 + b, :], 1.0, 0.0,
                                                           ALU.mult, ALU.add, ln_ss[:, j:j + 1])
                    then(ins)
                    dve.tensor_scalar(ln_ss[:, :], ln_ss[:, :], 1.0 / P, EPS, ALU.mult, ALU.add).then_inc(s.ln_ms, 1)
                    dve.wait_ge(s.ln_root, 1)
                    then(dve.reciprocal(ln_ss[:, :], ln_ss[:, :]))
                    for tt in range(TT):
                        for b in range(B_HEADS):
                            j = tt * B_HEADS + b
                            ins = dve.scalar_tensor_tensor(ob[:, tt, 4 + b, :], ob[:, tt, 4 + b, :], ln_ss[:, j:j + 1],
                                                           ln_g, ALU.mult, ALU.mult)
                    ins.then_inc(s.ocat, 1)
                for bank in range(KT // 2):
                    dve.wait_ge(s.o_tr, bank + 1)
                    dve.tensor_copy(hT[:, 2 * bank:2 * bank + 2, :],
                                    ps[:, bank, :].rearrange("p (k t) -> p k t", k=2)).then_inc(s.oT, 2)
                for tt in range(TT):
                    dve.wait_ge(s.mixed, tt + 1)
                    for half in range(2):
                        xs = x[:, tt, half * 512:(half + 1) * 512]
                        ins = dve.tensor_tensor(xs, ps[:, 4 + 2 * tt + half, :], xs, ALU.add)
                    ins.then_inc(s.x_mid, 1)
                norm(FFN[n])

                dve.wait_ge(ex.hT_hi, n + 1)
                dve.tensor_tensor(hT_lo[:, :, :], hT[:, :, :], hT_hi[:, :, :].bitcast(F32),
                                  ALU.subtract).then_inc(ex.hT_split, 1)

                per = 4 * 4 + 2 + 2 * 4 + 3

                with dve.Fori(0, HEADS) as i:
                    st = Steps(s.topk_step, i, per)
                    lanes = [(tt, c) for c in range(2) for tt in range(TT)]
                    top = {j: head_v[:, j[0], j[1], :] for j in lanes}
                    idx = {j: head_i[:, j[0], j[1], :] for j in lanes}
                    src = {j: ps[:, 6 + j[1], j[0] * P:(j[0] + 1) * P] for j in lanes}
                    k1, k2, k3 = {}, {}, {}
                    for j in lanes:
                        if j[0] == 0:
                            wait_apart(s.sc_ready[j[1]], done(i))
                        k1[j] = st.add(dve.max(top[j][:, 0:8], src[j]))
                    for j in lanes:
                        st.wait(k1[j])
                        k2[j] = st.add(dve.match_replace(left[:, j[1], j[0], :], top[j][:, 0:8], src[j], LOWEST))
                        ins = dve.max_index(idx[j][:, 0:8], top[j][:, 0:8], src[j])
                    ins.then_inc(s.sc_read, 1)
                    for j in lanes:
                        st.wait(k2[j])
                        k3[j] = st.add(dve.max(top[j][:, 8:16], left[:, j[1], j[0], :]))
                    for j in lanes:
                        st.wait(k3[j])
                        last = st.add(dve.max_index(idx[j][:, 8:16], top[j][:, 8:16], left[:, j[1], j[0], :]))
                    st.wait(last)
                    kc = {}
                    for tt in range(TT):
                        kc[tt] = st.add(dve.tensor_tensor(cand[:, tt],
                                                          top[tt, 0].unsqueeze(2).to_broadcast([P, TOPK, TOPK]),
                                                          top[tt, 1].unsqueeze(1).to_broadcast([P, TOPK, TOPK]), ALU.add))
                    flat = [cand[:, tt].rearrange("p a b -> p (a b)") for tt in range(TT)]
                    rest = [cand_left[:, tt].rearrange("p a b -> p (a b)") for tt in range(TT)]
                    best = [head_best[:, tt, :] for tt in range(TT)]
                    bidx = [head_j[:, tt, :] for tt in range(TT)]
                    for tt in range(TT):
                        st.wait(kc[tt])
                        k1[tt] = st.add(dve.max(best[tt][:, 0:8], flat[tt]))
                    for tt in range(TT):
                        st.wait(k1[tt])
                        dve.max_index(bidx[tt][:, 0:8], best[tt][:, 0:8], flat[tt])
                        k2[tt] = st.add(dve.match_replace(rest[tt], best[tt][:, 0:8], flat[tt], LOWEST))
                    for tt in range(TT):
                        st.wait(k2[tt])
                        k3[tt] = st.add(dve.max(best[tt][:, 8:16], rest[tt]))
                    for tt in range(TT):
                        st.wait(k3[tt])
                        ins = dve.max_index(bidx[tt][:, 8:16], best[tt][:, 8:16], rest[tt])
                        last = st.add(ins)
                    st.add(dve.tensor_copy(top_if[:, :, i, :, :], head_i))
                    st.add(dve.tensor_copy(best_v[:, :, i, :], head_best))
                    st.wait(last)
                    st.add(dve.tensor_copy(best_j[:, :, i, :], head_j))
                    assert st.n == per, st.n
                dve.wait_ge(s.topk_step, HEADS * per)

                groups = TT * HEADS
                bv = best_v.rearrange("p t h k -> p (t h) k")
                gate_out = picks[:, 2].rearrange("p t (h k) -> p (t h) k", h=HEADS)
                then(dve.tensor_tensor(gate_out, bv, bv[:, :, 0:1].to_broadcast([P, groups, TOPK]), ALU.subtract))
                dve.tensor_copy(bv, gate_out).then_inc(s.gate_d, 1)
                for c in range(2):
                    bj = best_j.rearrange("p t h k -> p (t h) k")
                    if c == 0:
                        then(dve.tensor_scalar(slot_i, bj, 4, None, ALU.logical_shift_right))
                    else:
                        then(dve.tensor_scalar(slot_i, bj, TOPK - 1, None, ALU.bitwise_and))
                    then(dve.tensor_copy(slot_f[:, c], slot_i))
                    then(dve.tensor_tensor(hit, slot_f[:, c].unsqueeze(3).to_broadcast([P, groups, TOPK, TOPK]),
                                           iota[:, 0:TOPK].unsqueeze(1).unsqueeze(1).to_broadcast([P, groups, TOPK, TOPK]),
                                           ALU.is_equal))
                    then(dve.tensor_tensor(hit, hit, top_if.rearrange("p t h c k -> p (t h) c k")[:, :, c, :].unsqueeze(2).to_broadcast([P, groups, TOPK, TOPK]),
                                           ALU.mult))
                    dve.tensor_reduce(picks[:, c].rearrange("p t (h k) -> p (t h) k", h=HEADS), hit, AX_X, ALU.add)
                dve.wait_ge(s.gate_e, 1)
                then(dve.tensor_reduce(gate_z, bv, AX_X, ALU.add))
                then(dve.reciprocal(gate_z, gate_z))
                dve.tensor_tensor(gate_out, bv, gate_z.unsqueeze(2).to_broadcast([P, groups, TOPK]),
                                  ALU.mult).then_inc(s.picked, 1)
                dve.wait_ge(s.picks_tr, 1)
                then(dve.tensor_copy(picksT[:, :, :].rearrange("p w t -> p (w t)"),
                                     ps[:, 4:6, :].rearrange("p b c -> p (b c)")[:, 0:3 * SEQ]))

                def rest_u(b, c):
                    dve.wait_ge(ex.u_hi, c + 1)
                    dve.tensor_tensor(u_lo[:, b], expert_u[:, b], u_hi[:, b].bitcast(F32),
                                      ALU.subtract).then_inc(ex.u_split, 1)

                def rest_v(b, c):
                    dve.wait_ge(ex.v_hi, c + 1)
                    dve.tensor_tensor(v_lo[:, b, :], expert_v[:, b, :], v_hi[:, b, :].bitcast(F32),
                                      ALU.subtract).then_inc(ex.v_split, 1)

                first = n * NKEYS
                rest_u(0, first)
                rest_u(1, first + 1)
                rest_v(0, first)

                with dve.Fori(0, SEQ // TOK_BODY) as i:
                    for g in range(2):
                        for j in range(TOK_HALF):
                            t = TOK_BODY * i + TOK_HALF * g + j
                            if g:
                                dve.wait_ge(s.gate_mm, TOK_BODY * i + j + 1)
                            else:
                                dve.wait_ge(s.gate_copied[1], free(i))
                            dve.tensor_scalar(onehot1[:, j, :], iota[:, :], picksT[:, 0, bass.ds(t, 1)],
                                              picksT[:, 2, bass.ds(t, 1)], ALU.is_equal, ALU.mult)
                            dve.tensor_scalar(onehot2[:, j, :], iota[:, :], picksT[:, 1, bass.ds(t, 1)],
                                              None, ALU.is_equal).then_inc(s.hot, 1)

                for g in range(2):
                    dve.wait_ge(s.gate_copied[g], free(SEQ // TOK_BODY))

                def weigh(b, c, key):
                    dve.wait_ge(ex.gelu, c + 1)
                    dve.tensor_tensor(weight[:, b, :], gelu_act[:, b, :], gate[:, key, :],
                                      ALU.mult).then_inc(ex.product, 1)
                    dve.wait_ge(ex.product, c + 1)
                    dve.tensor_copy(weight_hi[:, b, :], weight[:, b, :]).then_inc(ex.product_hi, 1)
                    dve.wait_ge(ex.product_hi, c + 1)
                    dve.tensor_tensor(weight_lo[:, b, :], weight[:, b, :], weight_hi[:, b, :].bitcast(F32),
                                      ALU.subtract).then_inc(ex.weighed, 1)

                weigh(0, first, 0)
                rest_u(0, first + 2)
                rest_v(1, first + 1)
                with dve.Fori(0, NKEYS // 2 - 2) as i:
                    for b, k in ((1, 1), (0, 2)):
                        c = first + 2 * i + k
                        weigh(b, c, 2 * i + k)
                        rest_u(b, c + 2)
                        rest_v(1 - b, c + 1)
                c = first + NKEYS - 3
                weigh(1, c, NKEYS - 3)
                rest_u(1, c + 2)
                rest_v(0, c + 1)
                weigh(0, c + 1, NKEYS - 2)
                rest_v(1, c + 2)
                weigh(1, c + 2, NKEYS - 1)
                dve.wait_ge(ex.summed, first + NKEYS)
                for half in range(2):
                    last = dve.tensor_copy(x[:, 0, half * 512:(half + 1) * 512], ps[:, half, :])
                last.then_inc(ex.x_end, 1)

            norm_scale(LAST)
            dve.wait_ge(s_fgain, 16)
            for tt in range(TT):
                ins = dve.scalar_tensor_tensor(h[:, tt, :], x[:, tt, :], rstd[:, tt:tt + 1], expert_v[:, 0, :],
                                               ALU.mult, ALU.mult)
            ins.then_inc(s_y, 1)


def _t5_bucket(dist):
    exact = BUCKETS // 2
    d = np.maximum(dist, 1).astype(np.float32)
    large = exact + (np.log(d / np.float32(exact)).astype(np.float32) / np.float32(math.log(MAX_DISTANCE / exact))
                     * np.float32(BUCKETS - exact)).astype(np.int32)
    return np.where(dist < exact, dist, np.minimum(large, BUCKETS - 1))


def _constants():
    dist = SEQ - 1 - np.arange(SPAN)
    bucket = _t5_bucket(np.maximum(dist, 0))
    onehot = (np.arange(BUCKETS)[:, None] == bucket[None, :]).astype(np.float32)
    mult = sum(((dist % d == 0) & (dist <= w)).astype(np.float64) for w, d in BRANCHES)
    row_a = np.where((dist >= 0) & (mult > 0), np.log(np.maximum(mult, 1)), MASKED)
    row_b = np.where(dist >= 0, 0.0, MASKED)
    rowmask = np.stack([row_a] * A_HEADS + [row_b] * B_HEADS).astype(np.float32)
    p, k = np.arange(P)[:, None], np.arange(SEQ)[None, :]
    mask8 = np.where(P + p - k >= 0, 0.0, MASKED / SCALE).astype(np.float32)
    tri = np.stack([(p + P * t <= k) for t in range(TT)], 1).astype(np.float32)
    iota = np.broadcast_to(np.arange(P, dtype=np.float32), (P, P)).copy()
    return {"c_bucket": onehot, "c_rowmask": rowmask, "c_mask8": mask8, "c_tri": tri, "c_iota": iota,
            "c_ident": np.eye(P, dtype=np.float32), "c_flip": np.eye(P, dtype=np.float32)[::-1]}


def _layout(v):
    def rows(w):
        return np.swapaxes(w.reshape(w.shape[:-2] + (KT, P, w.shape[-1])), -3, -2)

    def units(w, starts):
        return np.stack([np.concatenate([rows(w)[:, :, c:c + P] for c in cols], -1) for cols in starts])

    ev, od = v["even_w_in"][0], v["odd_w_in"][0]
    wa = A_HEADS * HEAD
    even = [(P * u, wa + P * u, 2 * wa + P * u) for u in range(4)] + \
           [(3 * wa + P * u, 3 * wa + wa + P * u, 3 * wa + 2 * wa + P * u) for u in range(4)]
    odd = [(P * u, D + P * u, 2 * D + P * u) for u in range(UNITS)]
    wq = v["peer_wq"]
    u = v["peer_u"].reshape(LAYERS, NKEYS, NKEYS, KT, P)
    return {
        "x": v["x"],
        "mix_g": np.swapaxes(v["norm_mix_g"].reshape(LAYERS, KT, P), 1, 2),
        "ffn_g": np.swapaxes(v["norm_ffn_g"].reshape(LAYERS, KT, P), 1, 2),
        "final_g": v["final_norm_g"],
        "rel_bias": v["rel_bias"],
        "diff_lambda": v["diff_lambda"].reshape(-1),
        "diff_ln_g": v["diff_ln_g"].reshape(-1),
        "odd_b_f": v["odd_b_f"].reshape(-1),
        "w_f": rows(od)[:, :, 3 * D:],
        "w_unit": np.stack([units(ev, even), units(od, odd)]),
        "w_out": np.stack([rows(v["even_w_out"][0]), rows(v["odd_w_out"][0])]),
        "w_query": np.transpose(wq.reshape(LAYERS, KT, P, HALVES, P), (0, 3, 2, 1, 4)),
        "subkeys": np.transpose(v["peer_subkeys"].reshape(LAYERS, HALVES, NKEYS, P), (0, 3, 1, 2)),
        "peer_u": np.transpose(u, (0, 2, 4, 3, 1)),
        "peer_v": v["peer_v"].reshape(LAYERS, NKEYS, NKEYS, D),
    }


def kernel(**inputs):
    import concourse.bacc as bacc
    from concourse.bass_utils import run_bass_kernel_spmd

    data = _layout({k: np.asarray(v) for k, v in inputs.items()})
    data.update(_constants())
    nc = bacc.Bacc("TRN2", target_bir_lowering=False, num_devices=1)
    arrays, aps = {}, {}
    for name, arr in data.items():
        arrays["in_" + name] = np.ascontiguousarray(arr)
        aps[name] = nc.dram_tensor("in_" + name, arr.shape, F32, kind="ExternalInput").ap()
    aps["y"] = nc.dram_tensor("out_y", (1, SEQ, D), F32, kind="ExternalOutput").ap()
    build(nc, aps)
    r = run_bass_kernel_spmd(nc, [arrays], core_ids=[0])
    return r.results[0]["out_y"]
```

```python
import math

import numpy as np
import concourse.bass as bass
from concourse import mybir
from contextlib import ExitStack

P = 128
D = 1024
KT = D // P
SEQ = 256
TT = SEQ // P
LAYERS = 2
A_HEADS, B_HEADS, C_HEADS = 8, 4, 16
BIAS_HEADS = A_HEADS + B_HEADS
BUCKETS, MAX_DISTANCE = 32, 2048
BRANCHES = ((128, 1), (512, 4), (2048, 16))
HEAD = 64
SCALE = HEAD ** -0.5
UNITS = D // P
UW = 3 * P
HEADS, TOPK, NKEYS = 8, 16, 128
HALVES = 2 * HEADS
SUM_BLOCKS = ((0, 1, 16), (1, 3, 8), (4, 12, 4))
SUMS_AT = tuple(sum(r * w for _, r, w in SUM_BLOCKS[:j]) for j in range(len(SUM_BLOCKS) + 1))
SUMS = SUMS_AT[-1]
EPS = 1e-6
LAM_INIT = 0.8 - 0.6 * math.exp(-0.3 * 0)
MASKED = -1e30
LOWEST = -3.0e38
SPAN = SEQ + P - 1
TOK_GROUP = 4
HOT_SLOTS = 4
AHEAD = 8
TOK_BODY = TOK_GROUP * HOT_SLOTS
TOK_HALF = TOK_BODY // 2

F32 = mybir.dt.float32
F32R = mybir.dt.float32r
BF16 = mybir.dt.bfloat16
U32 = mybir.dt.uint32
ALU = mybir.AluOpType
ACT = mybir.ActivationFunctionType
AX_X = mybir.AxisListType.X


class NormSems:

    def __init__(self, sem):
        self.sq = sem("norm_sumsq")
        self.ms = sem("norm_meansq")
        self.root = sem("norm_root")
        self.hn = sem("norm_scaled")
        self.tr = sem("norm_transposed")
        self.hT = sem("norm_hT")


class ExpertSems:

    def __init__(self, sem):
        self.unit_hi = sem("unit_hi_ready")
        self.unit_split = sem("unit_lo_ready")
        self.wq_hi = sem("wq_hi_ready")
        self.wq_split = sem("wq_lo_ready")
        self.u_loaded = [sem("u%d_loaded" % b) for b in range(2)]
        self.v_loaded = [sem("v%d_loaded" % b) for b in range(2)]
        self.u_hi = sem("u_hi_ready")
        self.u_split = sem("u_lo_ready")
        self.v_hi = sem("v_hi_ready")
        self.v_split = sem("v_lo_ready")
        self.hT_hi = sem("hT_hi_ready")
        self.hT_split = sem("hT_lo_ready")
        self.seeded = sem("residual_in_accumulators")
        self.act_ready = sem("act_ready")
        self.gelu = sem("gelu_ready")
        self.product = sem("weight_ready")
        self.product_hi = sem("weight_hi_ready")
        self.weighed = sem("weight_lo_ready")
        self.summed = sem("experts_summed")
        self.ended = sem("first_tile_summed")
        self.x_end = sem("x_after_ffn")


class LayerSems:

    def __init__(self, sem, p):
        self.w_loaded = [sem(p + "unit_w%d_loaded" % b) for b in range(2)]
        self.wo_loaded = sem(p + "w_out_loaded")
        self.qk_projected = sem(p + "qk_projected")
        self.v_projected = sem(p + "v_projected")
        self.qk_copied = sem(p + "qk_copied")
        self.v_copied = sem(p + "v_copied")
        self.scores = [sem(p + "scores%d" % m) for m in range(2)]
        self.max_ready = [sem(p + "max%d" % m) for m in range(2)]
        self.probs = [sem(p + "probs%d" % m) for m in range(2)]
        self.pt = [sem(p + "probsT%d" % m) for m in range(2)]
        self.pt_copied = [sem(p + "probsT_copied%d" % m) for m in range(2)]
        self.o_ready = sem(p + "o_ready")
        self.o_normed = sem(p + "o_normed")
        self.unit_step = sem(p + "dve_unit_steps")
        self.ln_ms = sem(p + "diff_ln_ms")
        self.ln_root = sem(p + "diff_ln_root")
        self.o_tr = sem(p + "o_transposed")
        self.oT = sem(p + "oT_ready")
        self.mixed = sem(p + "mixer_out")
        self.x_mid = sem(p + "x_after_mixer")
        self.sk_loaded = sem(p + "subkeys_loaded")
        self.wq_loaded = [sem(p + "wq%d_loaded" % c) for c in range(2)]
        self.q_ready = [sem(p + "q%d" % c) for c in range(2)]
        self.q_copied = [sem(p + "q%d_copied" % c) for c in range(2)]
        self.sc_ready = [sem(p + "sc%d" % c) for c in range(2)]
        self.sc_read = sem(p + "sc_read")
        self.topk_step = sem(p + "dve_topk_steps")
        self.gate_d = sem(p + "gate_logits")
        self.gate_e = sem(p + "gate_exps")
        self.picked = sem(p + "picks_ready")
        self.picks_tr = sem(p + "picks_transposed")
        self.picksT = sem(p + "picksT_ready")
        self.hot = sem(p + "onehots")
        self.gated = sem(p + "onehots_gated")
        self.gate_mm = sem(p + "gate_products")
        self.gate_copied = [sem(p + "gate_copied%d" % g) for g in range(2)]


def build(nc, a):
    with ExitStack() as ctx:
        def sb(name, shape, dt=F32):
            return ctx.enter_context(nc.sbuf_tensor(name, shape, dt))

        def sem(name):
            return ctx.enter_context(nc.semaphore(name))

        def next_offset():
            return -(-nc.sbuf_base // 32) * 32

        x_at = next_offset()
        x = sb("x", [P, TT, D])
        h_at = next_offset()
        h = sb("h", [P, TT, D])
        hT_at = next_offset()
        hT = sb("hT", [P, KT, SEQ])
        hT_lo = sb("hT_lo", [P, KT, SEQ], F32R)
        region = sb("region", [P, NKEYS * SEQ])
        expert_u_at = next_offset()
        expert_u = sb("expert_u", [P, 2, KT, P])
        expert_v_at = next_offset()
        expert_v = sb("expert_v", [P, 2, D])
        u_hi = sb("u_hi", [P, 2, KT, P], F32R)
        u_lo = sb("u_lo", [P, 2, KT, P], F32R)
        hot_at = [next_offset()]
        onehots = [sb("onehots0", [P, 2, TOK_GROUP, P])]
        hot_at.append(next_offset())
        onehots.append(sb("onehots1", [P, 2, TOK_GROUP, P]))
        v_hi = nc.alloc_sbuf_tensor_at("v_hi", [P, 2, D], F32R, offset=x_at)
        v_lo = nc.alloc_sbuf_tensor_at("v_lo", [P, 2, D], F32R, offset=hT_at)
        hT_hi = nc.alloc_sbuf_tensor_at("hT_hi", [P, KT, SEQ], F32R, offset=h_at)
        gelu_act = nc.alloc_sbuf_tensor_at("gelu_act", [P, 2, SEQ], F32, offset=hot_at[0])
        weight = nc.alloc_sbuf_tensor_at("weight", [P, 2, SEQ], F32, offset=hot_at[0] + 2 * SEQ * 4)
        weight_hi = nc.alloc_sbuf_tensor_at("weight_hi", [P, 2, SEQ], F32R, offset=hot_at[1])
        weight_lo = nc.alloc_sbuf_tensor_at("weight_lo", [P, 2, SEQ], F32R, offset=hot_at[1] + 2 * SEQ * 4)
        unit_hi = [u_hi, nc.alloc_sbuf_tensor_at("unit_hi1", [P, 2, KT, P], F32R, offset=expert_u_at)]
        unit_lo = [u_lo, nc.alloc_sbuf_tensor_at("unit_lo1", [P, 2, KT, P], F32R, offset=expert_v_at)]
        for j, offset in enumerate((x_at + D * 4, hT_at + D * 4)):
            onehots.append(nc.alloc_sbuf_tensor_at("onehots%d" % (2 + j), [P, 2, TOK_GROUP, P], F32, offset=offset))
        acts_ahead = sb("acts_ahead", [P, AHEAD, SEQ])
        picksT = sb("picksT", [P, 3, SEQ])
        ident = sb("ident", [P, P])
        iota = sb("iota", [P, P])
        gains = sb("gains", [P, 2 * LAYERS, KT])
        sumsq = sb("sumsq", [P, TT])
        rstd = sb("rstd", [P, TT])
        lam_in = sb("lam_in", [P, 4 * HEAD])
        lam = sb("lam", [P, 4])
        neg_max = sb("neg_max", [P, 2, TT])
        denom = sb("denom", [P, 2, TT])
        rdenom = sb("rdenom", [P, 2, TT])
        ln_ss = sb("ln_ss", [P, TT * B_HEADS])
        b_f = sb("b_f", [P, C_HEADS])
        w_f = sb("w_f", [P, KT, C_HEADS])
        logsig = sb("logsig", [P, TT, C_HEADS])
        lse_tmp = sb("lse_tmp", [P, TT, C_HEADS])
        cum8 = sb("cum8", [P, TT, C_HEADS])
        ps = ctx.enter_context(nc.psum_tensor("ps", [P, 8, 512], F32))

        gate = region[:, :].rearrange("p (i t) -> p i t", i=NKEYS)
        at = [0]

        def carve(shape, dt=F32):
            n = int(np.prod(shape)) // (2 if dt == BF16 else 1)
            v = region[:, at[0]:at[0] + n]
            at[0] += n
            assert at[0] <= NKEYS * SEQ
            if dt != F32:
                v = v.bitcast(dt)
            if len(shape) == 1:
                return v
            names = "abcdef"[:len(shape)]
            return v.rearrange("p (%s) -> p %s" % (" ".join(names), " ".join(names)),
                               **{c: s for c, s in zip(names, shape)})

        bias8 = carve([BIAS_HEADS, SEQ])
        cumT8 = carve([C_HEADS, SEQ])
        mask8 = carve([SEQ])
        h_mid = region[:, at[0]:at[0] + TT * D].rearrange("p (t d) -> p t d", t=TT)
        w_unit = carve([2, KT, UW])
        w_out = carve([KT, D])
        qkT = carve([2, 512])
        val = carve([2, TT, P])
        logits = carve([2, 384])
        probs = carve([2, 384])
        probsT = carve([2, 384])
        map_bias = carve([2, 384])
        tri = carve([TT, SEQ])
        ln_g = carve([P])
        row_in = carve([SPAN + 1])
        row_mask = carve([SPAN + 1])
        row_out = carve([SPAN + 1])
        cumT_row = carve([SEQ])
        o_sq = carve([TT * B_HEADS, P])
        flip = carve([P])
        o_rows = region[:, at[0]:at[0] + TT * D].rearrange("p (t d) -> p t d", t=TT)
        hankel = carve([BIAS_HEADS, SEQ])
        at[0] = 0
        subkeys = carve([HALVES, P])
        qTs = carve([2, SEQ])
        left = carve([2, TT, P])
        cand = carve([TT, SUMS])
        cand_left = carve([TT, SUMS])
        head_v = carve([TT, 2, TOPK])
        head_i = carve([TT, 2, TOPK]).bitcast(U32)
        head_best = carve([TT, TOPK])
        head_j = carve([TT, TOPK]).bitcast(U32)
        groups = TT * HEADS
        top_i = carve([2, TOPK, TT, HEADS], BF16)
        slot = carve([2, TOPK, groups], BF16)
        place = carve([TOPK, groups], BF16)
        hit = carve([2, TOPK, TOPK, groups], BF16)
        best_v = carve([TT, HEADS, TOPK])
        best_j = carve([TT, HEADS, TOPK]).bitcast(U32)
        step_i = carve([2, groups, TOPK]).bitcast(U32)
        step_f = carve([2, groups, TOPK])
        block1 = carve([groups, TOPK])
        column = carve([groups, TOPK])
        gate_z = carve([groups])
        picks = carve([3, TT, P])

        s_const = sem("const_loaded")
        s_row = sem("row_inputs_loaded")
        s_late = sem("late_constants_loaded")
        s_x = [sem("x%d_loaded" % tt) for tt in range(TT)]
        s_scratch = sem("bias_row_stored")
        s_bias = sem("bias_tiles_loaded")
        s_flip = sem("bias_tiles_flipped")
        s_flipped = sem("bias_tiles_ready")
        s_rowmm = sem("bias_row_product")
        s_rowdone = sem("bias_row_done")
        s_lamsum = sem("lambda_sums")
        s_lamexp = sem("lambda_exps")
        dve_straight = sem("dve_straight_steps")
        waited = sem("dve_waited_in_a_loop")
        act_straight = sem("act_straight_steps")
        s_fgw = sem("forget_weights_loaded")
        s_fg = sem("forget_logits")
        s_fgneg = sem("forget_neg_abs")
        s_fgln = sem("forget_ln")
        s_fglog = sem("forget_logsigmoid")
        s_cum = sem("forget_cumsum")
        s_cumrow = sem("forget_row_done")
        s_cumst = sem("forget_row_stored")
        s_cumld = sem("forget_tiles_loaded")
        s_fgain = sem("final_gain_loaded")
        s_y = sem("output_ready")
        s_out = sem("output_stored")

        MIX, FFN, LAST = [0, 2], [1, 3], 2 * LAYERS
        norms = NormSems(sem)
        ex = ExpertSems(sem)
        L = [LayerSems(sem, "L%d_" % n) for n in range(LAYERS)]

        bias_row = nc.dram_tensor("bias_row", (BIAS_HEADS, SPAN), F32, kind="Internal").ap()
        cum_row = nc.dram_tensor("cum_row", (C_HEADS, SEQ), F32, kind="Internal").ap()
        bias_src = bass.AP(tensor=bias_row.tensor, offset=0, ap=[[1, P], [SPAN, BIAS_HEADS], [1, SEQ]])
        CONSTS = 4 + 2 * LAYERS
        FLIP_BANKS = (6, 7, 0, 1, 2, 3)

        def free(u):
            return u + 1

        def done(u):
            return u + 2

        def credit(eng, *sems):
            for x in sems:
                eng.sem_inc(x, 1)

        def over_pairs(eng, n, body, before_last=None):
            if n == 0:
                with eng.Fori(0, 2) as i:
                    body("B", i, False)
                body("A", 2, False)
                if before_last:
                    before_last()
                body("A", 3, True)
            else:
                with eng.Fori(0, 3) as i:
                    body("C", i, False)
                body("C", 3, True)

        def summed(tt):
            return ps[:, 2 * tt:2 * tt + 2, :].rearrange("p b c -> p (b c)")

        def first_u(b):
            return expert_v[:, b, :].rearrange("p (k c) -> p k c", k=KT)

        def tile_half(t, tt, half):
            return t[:, 4 * half:4 * half + 4, tt * P:(tt + 1) * P]

        block = ctx.enter_context(nc.Block())

        @block.sync
        def _(sp):
            for tt in range(TT):
                sp.dma_start(x[:, tt, :], a["x"][0, tt * P:(tt + 1) * P, :]).then_inc(s_x[tt], 16)
            sp.dma_start(row_in[0:BUCKETS, 0:SPAN], a["c_bucket"]).then_inc(s_row, 16)
            sp.dma_start(row_out[0:BUCKETS, 0:BIAS_HEADS], a["rel_bias"]).then_inc(s_row, 16)
            sp.dma_start(row_mask[0:BIAS_HEADS, 0:SPAN], a["c_rowmask"]).then_inc(s_row, 16)
            sp.dma_start(ident[:, :], a["c_ident"]).then_inc(s_const, 16)
            sp.dma_start(flip, a["c_flip"]).then_inc(s_const, 16)
            for n in range(LAYERS):
                sp.dma_start(gains[:, 2 * n, :], a["mix_g"][n]).then_inc(s_const, 16)
                sp.dma_start(gains[:, 2 * n + 1, :], a["ffn_g"][n]).then_inc(s_const, 16)
            sp.dma_start(lam_in[:, :], a["diff_lambda"].partition_broadcast(P)).then_inc(s_const, 16)
            sp.dma_start(ln_g, a["diff_ln_g"].partition_broadcast(P)).then_inc(s_const, 16)
            for n in range(LAYERS):
                s = L[n]

                def load_unit(u):
                    sp.dma_start(w_unit[:, u, :, 2 * P:], a["w_value"][n, u]).then_inc(s.w_loaded[u], 16)
                    sp.dma_start(w_unit[:, u, :, 0:2 * P], a["w_qk"][n, u]).then_inc(s.w_loaded[u], 16)

                if n > 0:
                    sp.wait_ge(ex.product, n * NKEYS)
                load_unit(0)
                if n == 0:
                    sp.wait_ge(s_rowdone, 1)
                    sp.dma_start(bias_row, row_out[0:BIAS_HEADS, 0:SPAN]).then_inc(s_scratch, 16)
                    sp.wait_ge(s_scratch, 16)
                    sp.dma_start(hankel, bias_src).then_inc(s_bias, 16)
                    load_unit(1)
                    sp.dma_start(iota[:, :], a["c_iota"]).then_inc(s_late, 16)
                    sp.dma_start(b_f[:, :], a["odd_b_f"].partition_broadcast(P)).then_inc(s_late, 16)
                    sp.dma_start(w_f[:, :, :], a["w_f"]).then_inc(s_late, 16)
                else:
                    sp.dma_start(tri, a["c_tri"]).then_inc(s_fgw, 16)
                    sp.dma_start(mask8, a["c_mask8"]).then_inc(s_fgw, 16)
                    load_unit(1)
                    sp.wait_ge(s_cumrow, 1)
                    sp.dma_start(cum_row, cumT_row[0:C_HEADS, :]).then_inc(s_cumst, 16)
                    sp.wait_ge(s_cumst, 16)
                    sp.dma_start(cumT8, cum_row.rearrange("h t -> (h t)").partition_broadcast(P)
                                 .rearrange("p (h t) -> p h t", h=C_HEADS)).then_inc(s_cumld, 16)
                with sp.Fori(1, UNITS // 2) as i:
                    for b in range(2):
                        sp.wait_ge(s.v_projected, 2 * i + b - 1)
                        sp.dma_start(w_unit[:, b, :, 2 * P:], a["w_value"][n, 2 * i + b])\
                          .then_inc(s.w_loaded[b], 16)
                        sp.wait_ge(ex.unit_split, n * UNITS + 2 * i + b - 1)
                        sp.dma_start(w_unit[:, b, :, 0:2 * P], a["w_qk"][n, 2 * i + b])\
                          .then_inc(s.w_loaded[b], 16)
                sp.dma_start(w_out, a["w_out"][n]).then_inc(s.wo_loaded, 16)
                sp.wait_ge(s.qk_projected, UNITS)
                for c in range(2):
                    sp.dma_start(expert_u[:, c], a["w_query"][n, c]).then_inc(s.wq_loaded[c], 16)
                for b in range(2):
                    sp.dma_start(first_u(b), a["peer_u"][n, b]).then_inc(ex.u_loaded[b], 16)
                sp.wait_ge(s.x_mid, TT)
                sp.dma_start(subkeys, a["subkeys"][n]).then_inc(s.sk_loaded, 16)
                with sp.Fori(1, HEADS) as i:
                    for c in range(2):
                        sp.wait_ge(ex.wq_split, n * HALVES + 2 * (i - 1) + c + 1)
                        sp.dma_start(expert_u[:, c], a["w_query"][n, 2 * i + c]).then_inc(s.wq_loaded[c], 16)
                for b in range(2):
                    sp.wait_ge(ex.wq_split, (n + 1) * HALVES - 1 + b)
                    sp.dma_start(expert_u[:, b], a["peer_u"][n, 2 + b]).then_inc(ex.u_loaded[b], 16)
                for b in range(2):
                    sp.wait_ge(ex.u_split, n * NKEYS + b + 1)
                    sp.dma_start(expert_v[:, b, :], a["peer_v"][n][:, b, :]).then_inc(ex.v_loaded[b], 16)

                def reload_u(i, b):
                    sp.wait_ge(ex.u_split, n * NKEYS + 2 * (i - 1) + b + 1)
                    sp.dma_start(expert_u[:, b], a["peer_u"][n, 2 * i + b]).then_inc(ex.u_loaded[b], 16)

                def reload_v(i, b):
                    sp.wait_ge(ex.v_split, n * NKEYS + 2 * (i - 1) + b + 1)
                    sp.dma_start(expert_v[:, b, :], a["peer_v"][n][:, 2 * i + b, :]).then_inc(ex.v_loaded[b], 16)

                with sp.Fori(2, AHEAD // 2 + 1) as i:
                    for b in range(2):
                        reload_u(i, b)
                with sp.Fori(1, AHEAD // 2 + 1) as i:
                    for b in range(2):
                        reload_v(i, b)
                with sp.Fori(AHEAD // 2 + 1, NKEYS // 2) as i:
                    for b in range(2):
                        reload_u(i, b)
                        reload_v(i, b)
            sp.wait_ge(ex.v_split, LAYERS * NKEYS)
            sp.dma_start(expert_v[:, 0, :], a["final_g"].partition_broadcast(P)).then_inc(s_fgain, 16)
            for tt in range(TT):
                sp.wait_ge(s_y, tt + 1)
                sp.dma_start(a["y"][0, tt * P:(tt + 1) * P, :], h[:, tt, :]).then_inc(s_out, 16)
            sp.wait_ge(s_out, 16 * TT)

        @block.tensor
        def _(pe):
            def turn(src, tt, bank, done):
                for kt in range(KT):
                    c = (kt % 4) * P
                    last = pe.transpose(ps[:, bank + 2 * tt + kt // 4, c:c + P], src[:, tt, kt * P:(kt + 1) * P],
                                        ident[:, :])
                    if kt % 4 == 3:
                        last.then_inc(done, 1)

            def project_unit(s, n, b, u, i, after_values=None, before_keys=None):
                pe.wait_ge(s.w_loaded[b], 32 * (i + 1))
                pe.wait_ge(s.v_copied, free(u))
                for tt in range(TT):
                    for kt in range(KT):
                        last = pe.matmul(ps[:, 5, tt * P:(tt + 1) * P], hT[:, kt, tt * P:(tt + 1) * P],
                                         w_unit[:, b, kt, 2 * P:3 * P], start=(kt == 0), stop=(kt == KT - 1))
                last.then_inc(s.v_projected, 1)
                if after_values:
                    after_values()
                pe.wait_ge(s.qk_copied, free(u))
                pe.wait_ge(ex.unit_hi, n * UNITS + u + 1)
                pe.wait_ge(ex.hT_split, 2 * TT * (MIX[n] + 1))
                for part in range(2):
                    if part == 1 and before_keys:
                        before_keys()
                    out = ps[:, 4, part * SEQ:(part + 1) * SEQ]
                    for kt in range(KT):
                        for t in (hT_hi, hT_lo):
                            pe.matmul(out, unit_hi[b][:, part, kt, :], t[:, kt, :],
                                      start=(kt == 0 and t is hT_hi), stop=False)
                    if part == 0:
                        pe.wait_ge(ex.unit_split, n * UNITS + u + 1)
                    for kt in range(KT):
                        last = pe.matmul(out, unit_lo[b][:, part, kt, :], hT_hi[:, kt, :],
                                         start=False, stop=(kt == KT - 1))
                last.then_inc(s.qk_projected, 1)

            def attend(s, kind, b, u):
                pe.wait_ge(s.qk_copied, done(u))
                for m in range(2):
                    r = slice(m * HEAD, (m + 1) * HEAD)
                    pe.wait_ge(s.pt_copied[m], free(u))
                    pe.matmul(ps[:, 6 + m, 0:P], qkT[r, b, 0:P], qkT[r, b, SEQ:SEQ + P], start=True, stop=True)
                    pe.matmul(ps[:, 6 + m, P:3 * P], qkT[r, b, P:SEQ], qkT[r, b, SEQ:2 * SEQ],
                              start=True, stop=True).then_inc(s.scores[m], 1)

            def turn_probs(s, u):
                for m in range(2):
                    pe.wait_ge(s.probs[m], done(u))
                    for blk in range(3):
                        last = pe.transpose(ps[:, 6 + m, blk * P:(blk + 1) * P],
                                            probs[:, m, blk * P:(blk + 1) * P], ident[:, :])
                    last.then_inc(s.pt[m], 1)

            def combine(s, kind, b, u):
                pe.wait_ge(s.v_copied, done(u))
                pe.wait_ge(s.o_normed, free(u))
                w = P if kind == "B" else HEAD
                for m in range(2):
                    pe.wait_ge(s.pt_copied[m], done(u))
                    v0 = 0 if kind == "B" else m * HEAD
                    out = [ps[:, 0, (tt * 2 + m) * w:(tt * 2 + m + 1) * w] for tt in range(TT)]
                    pe.matmul(out[0], probsT[:, m, 0:P], val[:, b, 0, v0:v0 + w], start=True, stop=True)
                    pe.matmul(out[1], probsT[:, m, P:2 * P], val[:, b, 0, v0:v0 + w], start=True, stop=False)
                    last = pe.matmul(out[1], probsT[:, m, 2 * P:3 * P], val[:, b, 1, v0:v0 + w],
                                     start=False, stop=True)
                last.then_inc(s.o_ready, 1)

            for s in L:
                credit(pe, *s.pt, *s.sc_ready)
                pe.sem_inc(s.gate_mm, HOT_SLOTS)

            pe.wait_ge(s_row, 48)
            pe.matmul(ps[0:BIAS_HEADS, 5, 0:SPAN], row_out[0:BUCKETS, 0:BIAS_HEADS], row_in[0:BUCKETS, 0:SPAN],
                      start=True, stop=True).then_inc(s_rowmm, 1)
            pe.wait_ge(s_const, 16 * CONSTS)
            for n in range(LAYERS):
                s = L[n]
                if n == 0:
                    pe.wait_ge(s_rowdone, 1)
                for tt in range(TT):
                    pe.wait_ge(norms.hn, TT * MIX[n] + tt + 1)
                    turn(h, tt, 4, norms.tr)
                pe.wait_ge(norms.hT, 2 * TT * (MIX[n] + 1))
                if n > 0:
                    pe.wait_ge(ex.x_end, n)
                if n == 1:
                    pe.wait_ge(s_late, 48)
                    for tt in range(TT):
                        for kt in range(KT):
                            last = pe.matmul(ps[:, 2, tt * C_HEADS:(tt + 1) * C_HEADS],
                                             hT[:, kt, tt * P:(tt + 1) * P], w_f[:, kt, :],
                                             start=(kt == 0), stop=(kt == KT - 1))
                    last.then_inc(s_fg, 1)

                def cumulate():
                    pe.wait_ge(s_fglog, 1)
                    pe.wait_ge(s_fgw, 32)
                    for tt in range(TT):
                        for kt in range(TT):
                            pe.matmul(ps[:, 2, tt * C_HEADS:(tt + 1) * C_HEADS], tri[:, kt, tt * P:(tt + 1) * P],
                                      logsig[:, kt, :], start=(kt == 0), stop=(kt == TT - 1))
                    for kt in range(TT):
                        last = pe.matmul(ps[0:C_HEADS, 3, 0:SEQ], logsig[:, kt, :], tri[:, kt, :],
                                         start=(kt == 0), stop=(kt == TT - 1))
                    last.then_inc(s_cum, 1)

                project_unit(s, n, 0, 0, 0, cumulate if n == 1 else None)
                if n == 0:
                    pe.wait_ge(s_bias, 16)
                    for j, bank in enumerate(FLIP_BANKS):
                        pe.matmul(ps[:, bank, :], flip, hankel[:, 2 * j:2 * j + 2, :].rearrange("p h k -> p (h k)"),
                                  start=True, stop=True).then_inc(s_flip, 1)
                    pe.wait_ge(s_flipped, 2)
                def pair(kind, i, last_pair):
                    for b in range(2):
                        u = 2 * i + b
                        attend(s, kind, b, u)
                        if not (last_pair and b):
                            project_unit(s, n, 1 - b, u + 1, i + b, before_keys=lambda: turn_probs(s, u))
                        else:
                            turn_probs(s, u)
                        combine(s, kind, b, u)

                over_pairs(pe, n, pair)

                def mix(tt, half):
                    for kt in range(KT):
                        last = pe.matmul(ps[:, 4 + 2 * tt + half, :], hT[:, kt, tt * P:(tt + 1) * P],
                                         w_out[:, kt, half * 512:(half + 1) * 512],
                                         start=(kt == 0), stop=(kt == KT - 1))
                    last.then_inc(s.mixed, 1)

                pe.wait_ge(s.o_normed, free(UNITS))
                for tt in range(TT):
                    turn(o_rows, tt, 0, s.o_tr)
                pe.wait_ge(s.oT, 2)
                pe.wait_ge(s.wo_loaded, 16)
                mix(0, 0)
                mix(0, 1)
                pe.wait_ge(s.oT, 4)
                mix(1, 0)
                pe.wait_ge(norms.hn, TT * FFN[n] + 1)
                turn(h_mid, 0, 0, norms.tr)
                mix(1, 1)
                pe.wait_ge(norms.hn, TT * FFN[n] + 2)
                turn(h_mid, 1, 0, norms.tr)
                pe.wait_ge(norms.hT, 2 * TT * (FFN[n] + 1))
                pe.wait_ge(s.sk_loaded, 16)
                pe.wait_ge(ex.hT_split, 2 * TT * (FFN[n] + 1))
                with pe.Fori(0, HEADS) as i:
                    for c in range(2):
                        pe.wait_ge(ex.wq_hi, n * HALVES + 2 * i + c + 1)
                        pe.wait_ge(s.q_copied[c], free(i))
                        for kt in range(KT):
                            for t in (hT_hi, hT_lo):
                                pe.matmul(ps[:, 4 + c, 0:SEQ], u_hi[:, c, kt, :], t[:, kt, :],
                                          start=(kt == 0 and t is hT_hi), stop=False)
                        pe.wait_ge(ex.wq_split, n * HALVES + 2 * i + c + 1)
                        for kt in range(KT):
                            last = pe.matmul(ps[:, 4 + c, 0:SEQ], u_lo[:, c, kt, :], hT_hi[:, kt, :],
                                             start=False, stop=(kt == KT - 1))
                        last.then_inc(s.q_ready[c], 1)
                    for c in range(2):
                        pe.wait_ge(s.q_copied[c], done(i))
                        if c == 0:
                            pe.wait_ge(s.sc_read, free(i))
                        for tt in range(TT):
                            last = pe.matmul(ps[:, 6 + c, tt * P:(tt + 1) * P], qTs[:, c, tt * P:(tt + 1) * P],
                                             subkeys[:, 2 * i + c, :], start=True, stop=True)
                        last.then_inc(s.sc_ready[c], 1)

                for tt in range(TT):
                    for half in range(2):
                        last = pe.matmul(ps[:, 2 * tt + half, :], ident[:, :], x[:, tt, half * 512:(half + 1) * 512],
                                         start=True, stop=False)
                last.then_inc(ex.seeded, 1)

                first = n * NKEYS

                def experts_in(b, c, bank):
                    pe.wait_ge(ex.u_hi, c + 1)
                    for kt in range(KT):
                        for t in (hT_hi, hT_lo):
                            pe.matmul(ps[:, bank, 0:SEQ], u_hi[:, b, kt, :], t[:, kt, :],
                                      start=(kt == 0 and t is hT_hi), stop=False)
                    pe.wait_ge(ex.u_split, c + 1)
                    for kt in range(KT):
                        last = pe.matmul(ps[:, bank, 0:SEQ], u_lo[:, b, kt, :], hT_hi[:, kt, :],
                                         start=False, stop=(kt == KT - 1))
                    last.then_inc(ex.act_ready, 1)

                for b in range(2):
                    pe.wait_ge(s.q_copied[b], free(HEADS))
                    experts_in(b, first + b, 4 + b)
                with pe.Fori(1, AHEAD // 2) as i:
                    for b in range(2):
                        pe.wait_ge(ex.gelu, first + 2 * i + b - 1)
                        experts_in(b, first + 2 * i + b, 4 + b)

                pe.wait_ge(s.sc_read, free(HEADS))
                for w in range(3):
                    pe.wait_ge(s.picked, 1 + w // 2)
                    for tt in range(TT):
                        c = w * SEQ + tt * P
                        last = pe.transpose(ps[:, 6 + c // 512, c % 512:c % 512 + P], picks[:, w, tt, :], ident[:, :])
                    if w > 0:
                        last.then_inc(s.picks_tr, 1)

                pe.wait_ge(ex.gelu, first + AHEAD)
                pe.wait_ge(s.picksT, 2)
                with pe.Fori(0, SEQ // TOK_BODY) as i:
                    for g in range(HOT_SLOTS):
                        if g % 2 == 0:
                            pe.wait_ge(s.gate_copied[g // 2], free(i))
                        pe.wait_ge(s.gated, HOT_SLOTS * i + g + 1)
                        for j in range(TOK_GROUP):
                            last = pe.matmul(ps[:, 4 + g, j * P:(j + 1) * P], onehots[g][:, 0, j, :],
                                             onehots[g][:, 1, j, :], start=True, stop=True)
                        last.then_inc(s.gate_mm, 1)

                pe.wait_ge(s.gate_copied[0], free(SEQ // TOK_BODY))
                def experts_out(b, c, stop):
                    pe.wait_ge(ex.v_split, c + 1)
                    pe.wait_ge(ex.weighed, c + 1)
                    for tt in range(TT):
                        for w, v in ((weight_hi, v_hi), (weight_hi, v_lo), (weight_lo, v_hi)):
                            for half in range(2):
                                last = pe.matmul(ps[:, 2 * tt + half, :], w[:, b, tt * P:(tt + 1) * P],
                                                 v[:, b, half * 512:(half + 1) * 512], start=False,
                                                 stop=(stop and w is weight_lo))
                        if stop and tt == 0:
                            last.then_inc(ex.ended, 1)
                    last.then_inc(ex.summed, 1)

                experts_in(0, first + AHEAD, 4)
                with pe.Fori(0, AHEAD // 2) as i:
                    for b in range(2):
                        experts_out(b, first + 2 * i + b, False)
                with pe.Fori(AHEAD // 2, NKEYS // 2 - 1) as i:
                    c = first + 2 * i
                    experts_in(1, c + 1, 5)
                    experts_out(0, c, False)
                    experts_in(0, c + 2, 4)
                    experts_out(1, c + 1, False)
                c = first + NKEYS - 2
                experts_in(1, c + 1, 5)
                experts_out(0, c, False)
                experts_out(1, c + 1, True)

        @block.scalar
        def _(act):
            for s in L:
                credit(act, s.qk_copied, s.v_copied, *s.probs, *s.q_copied, *s.gate_copied)

            def norm(k, tt, src, junk, ready, ready_at):
                act.wait_ge(ready, ready_at)
                act.activation(junk[:, tt, :], src, ACT.Square, accum_out=sumsq[:, tt:tt + 1]).then_inc(norms.sq, 1)
                act.wait_ge(norms.ms, TT * k + tt + 1)
                act.activation(rstd[:, tt:tt + 1], sumsq[:, tt:tt + 1], ACT.Sqrt).then_inc(norms.root, 1)

            def round_hT(k, tt):
                for half in range(2):
                    act.wait_ge(norms.hT, 2 * TT * k + 2 * tt + half + 1)
                    act.copy(tile_half(hT_hi, tt, half), tile_half(hT, tt, half)).then_inc(ex.hT_hi, 1)

            def norm_sum(n):
                for tt, (ready, ready_at) in enumerate(((ex.ended, n), (ex.summed, n * NKEYS))):
                    norm(MIX[n] if n < LAYERS else LAST, tt, summed(tt), h, ready, ready_at)

            for n in range(LAYERS):
                s = L[n]
                if n == 0:
                    for tt in range(TT):
                        norm(MIX[0], tt, x[:, tt, :], h, s_x[tt], 16)
                else:
                    norm_sum(n)
                    for tt in range(TT):
                        act.wait_ge(norms.hn, TT * MIX[n] + tt + 1)
                        last = act.copy(x[:, tt, :], summed(tt))
                    last.then_inc(ex.x_end, 1)

                def round_unit(b, u, turn):
                    act.wait_ge(s.w_loaded[b], 32 * (turn + 1))
                    for part in range(2):
                        last = act.copy(unit_hi[b][:, part], w_unit[:, b, :, part * P:(part + 1) * P])
                    last.then_inc(ex.unit_hi, 1)

                round_unit(0, 0, 0)
                act.wait_ge(norms.tr, 2 * TT * (MIX[n] + 1))
                for tt in range(TT):
                    round_hT(MIX[n], tt)
                if n == 0:
                    act.wait_ge(s_lamsum, 1)
                    act.activation(lam[:, 2:4], lam[:, 0:2], ACT.Exp).then_inc(s_lamexp, 1)
                else:
                    act.wait_ge(s_fgneg, 1)
                    act.activation(lse_tmp[:, :, :], lse_tmp[:, :, :], ACT.Exp).then_inc(act_straight, 1)
                    act.wait_ge(s_fgneg, 2)
                    act.activation(lse_tmp[:, :, :], lse_tmp[:, :, :], ACT.Ln).then_inc(s_fgln, 1)

                def copy_unit(b, u):
                    act.wait_ge(s.v_projected, u + 1)
                    act.copy(val[:, b, :, :], ps[:, 5, 0:TT * P].rearrange("p (t c) -> p t c", t=TT))\
                       .then_inc(s.v_copied, 1)
                    act.wait_ge(s.qk_projected, u + 1)
                    act.copy(qkT[:, b, :], ps[:, 4, :]).then_inc(s.qk_copied, 1)

                def pair(kind, i, last_pair):
                    for b in range(2):
                        u = 2 * i + b
                        for m in range(2):
                            act.wait_ge(s.max_ready[m], u + 1)
                            act.wait_ge(s.pt[m], free(u))
                            act.wait_ge(s.o_normed, free(u))
                            act.activation(probs[:, m, 0:P], logits[:, m, 0:P], ACT.Exp,
                                           bias=neg_max[:, m, 0:1], scale=-1.0, accum_out=denom[:, m, 0:1])
                            act.activation(probs[:, m, P:3 * P], logits[:, m, P:3 * P], ACT.Exp,
                                           bias=neg_max[:, m, 1:2], scale=-1.0, accum_out=denom[:, m, 1:2])\
                               .then_inc(s.probs[m], 1)
                        if not last_pair:
                            round_unit(b, u + 2, i + 1)
                        if not (last_pair and b):
                            copy_unit(1 - b, u + 1)

                round_unit(1, 1, 0)
                copy_unit(0, 0)
                def diff_root():
                    act.wait_ge(s.ln_ms, 1)
                    act.activation(ln_ss[:, :], ln_ss[:, :], ACT.Sqrt).then_inc(s.ln_root, 1)

                over_pairs(act, n, pair, diff_root)

                def round_wq(c, i):
                    act.wait_ge(s.wq_loaded[c], 16 * (i + 1))
                    act.copy(u_hi[:, c], expert_u[:, c]).then_inc(ex.wq_hi, 1)

                def copy_query(c, i):
                    act.wait_ge(s.q_ready[c], i + 1)
                    act.wait_ge(s.sc_ready[c], free(i))
                    act.copy(qTs[:, c, :], ps[:, 4 + c, 0:SEQ]).then_inc(s.q_copied[c], 1)

                for c in range(2):
                    round_wq(c, 0)
                for tt in range(TT):
                    norm(FFN[n], tt, x[:, tt, :], h_mid, s.x_mid, tt + 1)
                    round_hT(FFN[n], tt)

                with act.Fori(0, HEADS - 1) as i:
                    for c in range(2):
                        copy_query(c, i)
                        round_wq(c, i + 1)
                for c in range(2):
                    copy_query(c, HEADS - 1)
                def round_u(b, c, turn, src=None):
                    act.wait_ge(ex.u_loaded[b], 16 * (turn + 1))
                    act.copy(u_hi[:, b], src or expert_u[:, b]).then_inc(ex.u_hi, 1)

                def round_v(b, c, turn):
                    act.wait_ge(ex.v_loaded[b], 16 * (turn + 1))
                    act.copy(v_hi[:, b, :], expert_v[:, b, :]).then_inc(ex.v_hi, 1)

                first, turn0 = n * NKEYS, n * NKEYS // 2
                for b in range(2):
                    round_u(b, first + b, turn0, first_u(b))

                def activate_ahead(b, k, i, more=True):
                    act.wait_ge(ex.act_ready, first + k + 1)
                    if more:
                        round_u(b, first + k + 2, turn0 + i + 1)
                    act.activation(acts_ahead[:, k, :], ps[:, 4 + b, 0:SEQ], ACT.Gelu).then_inc(ex.gelu, 1)

                for b in range(2):
                    activate_ahead(b, b, 0)
                act.wait_ge(s.gate_d, 1)
                act.activation(best_v, best_v, ACT.Exp).then_inc(s.gate_e, 1)
                for k in range(2, AHEAD):
                    activate_ahead(k % 2, k, k // 2, more=(k < AHEAD - 2))
                act.wait_ge(s.picks_tr, 1)
                act.copy(picksT[:, 0:2, :].rearrange("p w t -> p (w t)"), ps[:, 6, :]).then_inc(s.picksT, 1)
                act.wait_ge(s.picks_tr, 2)
                act.copy(picksT[:, 2, :], ps[:, 7, 0:SEQ]).then_inc(s.picksT, 1)

                act.wait_ge(ex.seeded, n + 1)
                round_v(0, first, turn0)
                for b in range(2):
                    round_u(b, first + AHEAD + b, turn0 + AHEAD // 2)

                with act.Fori(0, SEQ // TOK_BODY) as i:
                    for g in range(2):
                        act.wait_ge(s.gate_mm, HOT_SLOTS * i + 2 * (g + 1) + HOT_SLOTS)
                        act.copy(gate[:, :, bass.ds(TOK_BODY * i + TOK_HALF * g, TOK_HALF)],
                                 ps[:, 4 + 2 * g:6 + 2 * g, :].rearrange("p b (t i) -> p i (b t)", t=4))\
                           .then_inc(s.gate_copied[g], 1)

                def activate(b, c):
                    act.wait_ge(ex.act_ready, c + 1)
                    act.activation(gelu_act[:, b, :], ps[:, 4 + b, 0:SEQ], ACT.Gelu).then_inc(ex.gelu, 1)

                round_v(1, first + 1, turn0)
                activate(0, first + AHEAD)
                with act.Fori(0, AHEAD // 2) as i:
                    for b in range(2):
                        c = first + 2 * i + b + 1
                        act.wait_ge(ex.summed, c)
                        round_v(b, c + 1, turn0 + i + 1)
                round_u(0, first + AHEAD + 2, turn0 + AHEAD // 2 + 1)
                with act.Fori(AHEAD // 2, NKEYS // 2 - 2) as i:
                    c = first + 2 * i + 1
                    for b in (1, 0):
                        activate(b, c)
                        round_u(b, c + 2, turn0 + i + 1 + (1 - b))
                        act.wait_ge(ex.summed, c)
                        round_v(1 - b, c + 1, turn0 + i + 1)
                        c = c + 1
                c = first + NKEYS - 3
                activate(1, c)
                round_u(1, c + 2, turn0 + NKEYS // 2 - 1)
                act.wait_ge(ex.summed, c)
                round_v(0, c + 1, turn0 + NKEYS // 2 - 1)
                activate(0, c + 1)
                act.wait_ge(ex.summed, c + 1)
                round_v(1, c + 2, turn0 + NKEYS // 2 - 1)
                activate(1, c + 2)
            norm_sum(LAYERS)

        @block.vector
        def _(dve):
            straight = [0]

            def then(ins):
                straight[0] += 1
                ins.then_inc(dve_straight, 1)
                dve.wait_ge(dve_straight, straight[0])

            def wait_apart(sem, value):
                dve.wait_ge(sem, value)
                dve.sem_inc(waited, 1)

            class Steps:

                def __init__(self, sem, turns, per):
                    self.sem, self.base, self.n = sem, turns * per, 0

                def add(self, ins):
                    self.n += 1
                    ins.then_inc(self.sem, 1)
                    return self.n

                def wait(self, k):
                    wait_apart(self.sem, self.base + k)

            def norm_root(k, tt):
                dve.wait_ge(norms.sq, TT * k + tt + 1)
                dve.tensor_scalar(sumsq[:, tt:tt + 1], sumsq[:, tt:tt + 1], 1.0 / D, EPS, ALU.mult,
                                  ALU.add).then_inc(norms.ms, 1)
                dve.wait_ge(norms.root, TT * k + tt + 1)
                then(dve.reciprocal(rstd[:, tt:tt + 1], rstd[:, tt:tt + 1]))

            def norm_scale(k, tt, src, dst):
                norm_root(k, tt)
                dve.tensor_scalar(dst[:, tt, :], src, rstd[:, tt:tt + 1], None, ALU.mult).then_inc(norms.hn, 1)

            def norm_turned(k, tt, bank):
                for half in range(2):
                    dve.wait_ge(norms.tr, 2 * TT * k + 2 * tt + half + 1)
                    dve.tensor_tensor(tile_half(hT, tt, half),
                                      ps[:, bank + 2 * tt + half, :].rearrange("p (k t) -> p k t", k=4),
                                      gains[:, k, 4 * half:4 * half + 4].unsqueeze(2).to_broadcast([P, 4, P]),
                                      ALU.mult).then_inc(norms.hT, 1)

            def rest_hT(k, tt):
                for half in range(2):
                    dve.wait_ge(ex.hT_hi, 2 * TT * k + 2 * tt + half + 1)
                    dve.tensor_tensor(tile_half(hT_lo, tt, half), tile_half(hT, tt, half),
                                      tile_half(hT_hi, tt, half).bitcast(F32), ALU.subtract).then_inc(ex.hT_split, 1)

            for s in L:
                credit(dve, *s.pt_copied, s.o_normed, s.sc_read)

            dve.wait_ge(s_rowmm, 1)
            then(dve.tensor_tensor(row_mask[0:BIAS_HEADS, 0:SPAN], ps[0:BIAS_HEADS, 5, 0:SPAN],
                                   row_mask[0:BIAS_HEADS, 0:SPAN], ALU.add))
            dve.tensor_scalar(row_out[0:BIAS_HEADS, 0:SPAN], row_mask[0:BIAS_HEADS, 0:SPAN], 1.0 / SCALE, None,
                              ALU.mult).then_inc(s_rowdone, 1)
            dve.wait_ge(s_const, 16 * CONSTS)
            for j in range(2):
                last = dve.tensor_tensor_reduce(lam_in[:, 2 * j * HEAD:(2 * j + 1) * HEAD],
                                                lam_in[:, 2 * j * HEAD:(2 * j + 1) * HEAD],
                                                lam_in[:, (2 * j + 1) * HEAD:(2 * j + 2) * HEAD], 1.0, 0.0,
                                                ALU.mult, ALU.add, lam[:, j:j + 1])
            last.then_inc(s_lamsum, 1)

            for n in range(LAYERS):
                s = L[n]
                for tt in range(TT):
                    norm_scale(MIX[n], tt, x[:, tt, :] if n == 0 else summed(tt), h)
                for tt in range(TT):
                    norm_turned(MIX[n], tt, 4)
                for tt in range(TT):
                    rest_hT(MIX[n], tt)
                if n == 0:
                    dve.wait_ge(s_lamexp, 1)
                    then(dve.tensor_tensor(lam[:, 0:1], lam[:, 3:4], lam[:, 2:3], ALU.subtract))
                    then(dve.tensor_scalar(lam[:, 0:1], lam[:, 0:1], -LAM_INIT, None, ALU.add))
                    then(dve.tensor_scalar(ln_g, ln_g, 1.0 - LAM_INIT, None, ALU.mult))
                    for j, bank in enumerate(FLIP_BANKS):
                        dve.wait_ge(s_flip, j + 1)
                        dve.tensor_copy(bias8[:, 2 * j:2 * j + 2, :],
                                        ps[:, bank, :].rearrange("p (h k) -> p h k", h=2)).then_inc(s_flipped, 1)
                    dve.wait_ge(s_flipped, len(FLIP_BANKS))
                else:
                    dve.wait_ge(s_fg, 1)
                    fg = ps[:, 2, 0:TT * C_HEADS].rearrange("p (t h) -> p t h", t=TT)
                    for tt in range(TT):
                        ins = dve.tensor_tensor(logsig[:, tt, :], fg[:, tt, :], b_f[:, :], ALU.add)
                    then(ins)
                    dve.scalar_tensor_tensor(lse_tmp[:, :, :], logsig[:, :, :], -1.0, logsig[:, :, :], ALU.mult, ALU.min)\
                       .then_inc(s_fgneg, 1)
                    then(dve.tensor_scalar(logsig[:, :, :], logsig[:, :, :], 0.0, None, ALU.min))
                    dve.wait_ge(act_straight, 1)
                    dve.tensor_scalar(lse_tmp[:, :, :], lse_tmp[:, :, :], 1.0, None, ALU.add).then_inc(s_fgneg, 1)
                    dve.wait_ge(s_fgln, 1)
                    dve.tensor_tensor(logsig[:, :, :], logsig[:, :, :], lse_tmp[:, :, :], ALU.subtract)\
                       .then_inc(s_fglog, 1)
                    dve.wait_ge(s_cum, 1)
                    dve.tensor_scalar(cumT_row[0:C_HEADS, :], ps[0:C_HEADS, 3, 0:SEQ], -1.0 / SCALE, None,
                                      ALU.mult).then_inc(s_cumrow, 1)
                    then(dve.tensor_scalar(cum8[:, :, :], fg, 1.0 / SCALE, None, ALU.mult))
                    dve.wait_ge(s_fgw, 32)
                    dve.wait_ge(s_cumld, 16)

                steps_per_unit = {"A": 3, "B": 5, "C": 3}

                def pair(kind, i, last_pair):
                    st = Steps(s.unit_step, i, 2 * steps_per_unit[kind])
                    if kind == "A":
                        st.base = B_HEADS * steps_per_unit["B"] + (i - B_HEADS // 2) * 2 * steps_per_unit["A"]
                    for b in range(2):
                        u = 2 * i + b
                        for m in range(2):
                            if kind == "C":
                                hd = 2 * u + m
                                dve.scalar_tensor_tensor(map_bias[:, m, 0:P], cumT8[:, hd, 0:P], cum8[:, 0, bass.ds(hd, 1)],
                                                         mask8[:, P:SEQ], ALU.add, ALU.add)
                                k = st.add(dve.scalar_tensor_tensor(map_bias[:, m, P:3 * P], cumT8[:, hd, :],
                                                                    cum8[:, 1, bass.ds(hd, 1)],
                                                                    mask8, ALU.add, ALU.add))
                                t0 = map_bias[:, m, 0:P]
                            else:
                                hd = 2 * (u - B_HEADS) + m if kind == "A" else u + A_HEADS
                                k = st.add(dve.tensor_copy(map_bias[:, m, P:3 * P], bias8[:, hd, :]))
                                t0 = map_bias[:, m, 2 * P:3 * P]
                            t1 = map_bias[:, m, P:3 * P]
                            st.wait(k)
                            dve.wait_ge(s.scores[m], u + 1)
                            wait_apart(s.probs[m], free(u))
                            dve.tensor_tensor_reduce(logits[:, m, 0:P], ps[:, 6 + m, 0:P], t0, -SCALE, -LOWEST,
                                                     ALU.add, ALU.min, neg_max[:, m, 0:1])
                            dve.tensor_tensor_reduce(logits[:, m, P:3 * P], ps[:, 6 + m, P:3 * P], t1, -SCALE,
                                                     -LOWEST, ALU.add, ALU.min, neg_max[:, m, 1:2])\
                               .then_inc(s.max_ready[m], 1)
                        for m in range(2):
                            dve.wait_ge(s.pt[m], done(u))
                            dve.tensor_copy(probsT[:, m, :], ps[:, 6 + m, 0:3 * P]).then_inc(s.pt_copied[m], 1)
                        k = st.add(dve.reciprocal(rdenom[:, :, :], denom[:, :, :]))
                        st.wait(k)
                        dve.wait_ge(s.o_ready, u + 1)
                        if kind == "B":
                            k = st.add(dve.tensor_scalar(rdenom[:, 1, :], rdenom[:, 1, :], lam[:, 0:1], None, ALU.mult))
                            st.wait(k)
                            hu = o_rows.rearrange("p t (u c) -> p t u c", u=UNITS)[:, :, u, :]
                            for tt in range(TT):
                                ins = dve.tensor_scalar(hu[:, tt, :], ps[:, 0, tt * 2 * P:(tt * 2 + 1) * P],
                                                        rdenom[:, 0, tt:tt + 1], None, ALU.mult)
                            k = st.add(ins)
                            st.wait(k)
                            for tt in range(TT):
                                ins = dve.scalar_tensor_tensor(hu[:, tt, :], ps[:, 0, (tt * 2 + 1) * P:(tt * 2 + 2) * P],
                                                               rdenom[:, 1, tt:tt + 1], hu[:, tt, :], ALU.mult, ALU.add)
                        else:
                            hu = o_rows.rearrange("p t (u m c) -> p t u m c", u=UNITS, m=2)
                            for m in range(2):
                                for tt in range(TT):
                                    ins = dve.tensor_scalar(hu[:, tt, u, m, :],
                                                            ps[:, 0, (tt * 2 + m) * HEAD:(tt * 2 + m + 1) * HEAD],
                                                            rdenom[:, m, tt:tt + 1], None, ALU.mult)
                        ins.then_inc(s.o_normed, 1)
                    assert st.n == 2 * steps_per_unit[kind]

                def diff_norm():
                    dve.wait_ge(s.o_normed, free(UNITS - 2))
                    ob = o_rows.rearrange("p t (u c) -> p t u c", u=UNITS)
                    for tt in range(TT):
                        for b in range(B_HEADS):
                            j = tt * B_HEADS + b
                            ins = dve.tensor_tensor_reduce(o_sq[:, j, :], ob[:, tt, b, :], ob[:, tt, b, :], 1.0, 0.0,
                                                           ALU.mult, ALU.add, ln_ss[:, j:j + 1])
                    then(ins)
                    dve.tensor_scalar(ln_ss[:, :], ln_ss[:, :], 1.0 / P, EPS, ALU.mult, ALU.add).then_inc(s.ln_ms, 1)
                    dve.wait_ge(s.ln_root, 1)
                    then(dve.reciprocal(ln_ss[:, :], ln_ss[:, :]))
                    for tt in range(TT):
                        for b in range(B_HEADS):
                            j = tt * B_HEADS + b
                            ins = dve.scalar_tensor_tensor(ob[:, tt, b, :], ob[:, tt, b, :], ln_ss[:, j:j + 1],
                                                           ln_g, ALU.mult, ALU.mult)

                over_pairs(dve, n, pair, diff_norm)
                for tt in range(TT):
                    for half in range(2):
                        dve.wait_ge(s.o_tr, 2 * tt + half + 1)
                        dve.tensor_copy(tile_half(hT, tt, half),
                                        ps[:, 2 * tt + half, :].rearrange("p (k t) -> p k t", k=4)).then_inc(s.oT, 1)

                def add_mixed(tt, half):
                    dve.wait_ge(s.mixed, 2 * tt + half + 1)
                    xs = x[:, tt, half * 512:(half + 1) * 512]
                    return dve.tensor_tensor(xs, ps[:, 4 + 2 * tt + half, :], xs, ALU.add)

                if n > 0:
                    dve.wait_ge(ex.x_end, n)
                add_mixed(0, 0)
                add_mixed(0, 1).then_inc(s.x_mid, 1)
                norm_scale(FFN[n], 0, x[:, 0, :], h_mid)
                add_mixed(1, 0)
                norm_turned(FFN[n], 0, 0)
                rest_hT(FFN[n], 0)
                add_mixed(1, 1).then_inc(s.x_mid, 1)
                norm_scale(FFN[n], 1, x[:, 1, :], h_mid)
                norm_turned(FFN[n], 1, 0)
                rest_hT(FFN[n], 1)

                dve.wait_ge(s_late, 48)
                dve.tensor_copy(place, iota[:, 0:TOPK].unsqueeze(2).to_broadcast([P, TOPK, groups]))

                per = 4 * 4 + len(SUM_BLOCKS) + 2 * 4 + 3

                def search(st, i):
                    lanes = [(tt, c) for c in range(2) for tt in range(TT)]
                    top = {j: head_v[:, j[0], j[1], :] for j in lanes}
                    idx = {j: head_i[:, j[0], j[1], :] for j in lanes}
                    src = {j: ps[:, 6 + j[1], j[0] * P:(j[0] + 1) * P] for j in lanes}
                    k1, k2, k3 = {}, {}, {}
                    for j in lanes:
                        if j[0] == 0:
                            wait_apart(s.sc_ready[j[1]], done(i))
                        k1[j] = st.add(dve.max(top[j][:, 0:8], src[j]))
                    for j in lanes:
                        st.wait(k1[j])
                        k2[j] = st.add(dve.match_replace(left[:, j[1], j[0], :], top[j][:, 0:8], src[j], LOWEST))
                        ins = dve.max_index(idx[j][:, 0:8], top[j][:, 0:8], src[j])
                    ins.then_inc(s.sc_read, 1)
                    for j in lanes:
                        st.wait(k2[j])
                        k3[j] = st.add(dve.max(top[j][:, 8:16], left[:, j[1], j[0], :]))
                    for j in lanes:
                        st.wait(k3[j])
                        last = st.add(dve.max_index(idx[j][:, 8:16], top[j][:, 8:16], left[:, j[1], j[0], :]))
                    for (a0, rows, cols), at0 in zip(SUM_BLOCKS, SUMS_AT):
                        shape = [P, TT, rows, cols]
                        kc = st.add(dve.tensor_tensor(cand[:, :, at0:at0 + rows * cols].rearrange("p t (a b) -> p t a b", b=cols),
                                                      head_v[:, :, 0, a0:a0 + rows].unsqueeze(3).to_broadcast(shape),
                                                      head_v[:, :, 1, 0:cols].unsqueeze(2).to_broadcast(shape), ALU.add))
                    st.wait(last)
                    st.add(dve.tensor_copy(top_i[:, :, :, :, i].rearrange("p c k t -> p t c k"), head_i))
                    flat = [cand[:, tt] for tt in range(TT)]
                    rest = [cand_left[:, tt] for tt in range(TT)]
                    best = [head_best[:, tt, :] for tt in range(TT)]
                    bidx = [head_j[:, tt, :] for tt in range(TT)]
                    st.wait(kc)
                    for tt in range(TT):
                        k1[tt] = st.add(dve.max(best[tt][:, 0:8], flat[tt]))
                    for tt in range(TT):
                        st.wait(k1[tt])
                        k2[tt] = st.add(dve.match_replace(rest[tt], best[tt][:, 0:8], flat[tt], LOWEST))
                    for tt in range(TT):
                        dve.max_index(bidx[tt][:, 0:8], best[tt][:, 0:8], flat[tt])
                    for tt in range(TT):
                        st.wait(k2[tt])
                        k3[tt] = st.add(dve.max(best[tt][:, 8:16], rest[tt]))
                    for tt in range(TT):
                        st.wait(k3[tt])
                        last = st.add(dve.max_index(bidx[tt][:, 8:16], best[tt][:, 8:16], rest[tt]))
                    st.add(dve.tensor_copy(best_v[:, :, i, :], head_best))
                    st.wait(last)
                    st.add(dve.tensor_copy(best_j[:, :, i, :], head_j))

                with dve.Fori(0, HEADS // 2) as i:
                    st = Steps(s.topk_step, i, 2 * per)
                    search(st, 2 * i)
                    search(st, 2 * i + 1)
                    assert st.n == 2 * per, st.n
                dve.wait_ge(s.topk_step, HEADS * per)

                bv = best_v.rearrange("p t h k -> p (t h) k")
                bj = best_j.rearrange("p t h k -> p (t h) k")
                gate_out = picks[:, 2].rearrange("p t (h k) -> p (t h) k", h=HEADS)
                then(dve.tensor_tensor(gate_out, bv, bv[:, :, 0:1].to_broadcast([P, groups, TOPK]), ALU.subtract))
                dve.tensor_copy(bv, gate_out).then_inc(s.gate_d, 1)
                for j in range(2):
                    dve.tensor_scalar(step_i[:, j], bj, SUMS_AT[j + 1], SUMS_AT[j + 1], ALU.max, ALU.subtract)
                dve.tensor_scalar(block1, bj, float(SUMS_AT[1]), 8.0, ALU.is_ge, ALU.mult)
                then(dve.tensor_copy(column, bj))
                dve.tensor_scalar(step_i[:, 0], step_i[:, 0], 3, None, ALU.logical_shift_right)
                dve.tensor_scalar(step_i[:, 1], step_i[:, 1], 2, None, ALU.logical_shift_right)
                then(dve.tensor_tensor(column, column, block1, ALU.subtract))
                dve.tensor_scalar(step_f[:, 0], step_i[:, 0], float(SUM_BLOCKS[1][1]), None, ALU.min)
                then(dve.tensor_scalar(step_f[:, 1], step_i[:, 1], 4.0, None, ALU.mult))
                then(dve.scalar_tensor_tensor(block1, block1, 1.0 / 8, step_f[:, 0], ALU.mult, ALU.add))
                dve.scalar_tensor_tensor(column, block1, -8.0, column, ALU.mult, ALU.add)
                then(dve.scalar_tensor_tensor(slot[:, 0].rearrange("p k m -> p m k"), step_f[:, 1], 1.0 / 4, block1,
                                              ALU.mult, ALU.add))
                then(dve.tensor_tensor(slot[:, 1].rearrange("p k m -> p m k"), column, step_f[:, 1], ALU.subtract))
                shape = [P, TOPK, TOPK, groups]
                for c in range(2):
                    ins = dve.tensor_tensor(hit[:, c], slot[:, c].unsqueeze(1).to_broadcast(shape),
                                            place.unsqueeze(2).to_broadcast(shape), ALU.is_equal)
                then(ins)
                for c in range(2):
                    ins = dve.tensor_tensor(hit[:, c], hit[:, c],
                                            top_i[:, c].rearrange("p k t h -> p k (t h)").unsqueeze(2)
                                            .to_broadcast(shape), ALU.mult)
                then(ins)
                k = TOPK // 2
                while k > 1:
                    then(dve.tensor_tensor(hit[:, :, 0:k], hit[:, :, 0:k], hit[:, :, k:2 * k], ALU.add))
                    k //= 2
                for c in range(2):
                    ins = dve.tensor_tensor(picks[:, c].rearrange("p t (h k) -> p k (t h)", h=HEADS),
                                            hit[:, c, 0], hit[:, c, 1], ALU.add)
                ins.then_inc(s.picked, 1)
                dve.wait_ge(s.gate_e, 1)
                then(dve.tensor_reduce(gate_z, bv, AX_X, ALU.add))
                then(dve.reciprocal(gate_z, gate_z))
                dve.tensor_tensor(gate_out, bv, gate_z.unsqueeze(2).to_broadcast([P, groups, TOPK]),
                                  ALU.mult).then_inc(s.picked, 1)
                def rest_u(b, c):
                    dve.wait_ge(ex.u_hi, c + 1)
                    dve.tensor_tensor(u_lo[:, b], expert_u[:, b], u_hi[:, b].bitcast(F32),
                                      ALU.subtract).then_inc(ex.u_split, 1)

                def rest_v(b, c):
                    dve.wait_ge(ex.v_hi, c + 1)
                    dve.tensor_tensor(v_lo[:, b, :], expert_v[:, b, :], v_hi[:, b, :].bitcast(F32),
                                      ALU.subtract).then_inc(ex.v_split, 1)

                first = n * NKEYS
                dve.wait_ge(s.picksT, 1)
                dve.wait_ge(ex.seeded, n + 1)
                with dve.Fori(0, SEQ // TOK_BODY) as i:
                    for g in range(HOT_SLOTS):
                        dve.wait_ge(s.gate_mm, HOT_SLOTS * i + g + 1)
                        t = TOK_BODY * i + TOK_GROUP * g
                        shape = [P, 2, TOK_GROUP, P]
                        dve.tensor_tensor(onehots[g][:, :, :, :],
                                          iota[:, :].unsqueeze(1).unsqueeze(1).to_broadcast(shape),
                                          picksT[:, 0:2, bass.ds(t, TOK_GROUP)].unsqueeze(3).to_broadcast(shape),
                                          ALU.is_equal).then_inc(s.hot, 1)

                rest_u(0, first + AHEAD)
                rest_v(0, first)

                for g in range(2):
                    dve.wait_ge(s.gate_copied[g], free(SEQ // TOK_BODY))

                def weigh(b, c, key, act):
                    dve.wait_ge(ex.gelu, c + 1)
                    dve.tensor_tensor(weight[:, b, :], act, gate[:, key, :], ALU.mult).then_inc(ex.product, 1)
                    dve.wait_ge(ex.product, c + 1)
                    dve.tensor_copy(weight_hi[:, b, :], weight[:, b, :]).then_inc(ex.product_hi, 1)
                    dve.wait_ge(ex.product_hi, c + 1)
                    dve.tensor_tensor(weight_lo[:, b, :], weight[:, b, :], weight_hi[:, b, :].bitcast(F32),
                                      ALU.subtract).then_inc(ex.weighed, 1)

                for b in range(2):
                    weigh(b, first + b, b, acts_ahead[:, b, :])
                    if b == 0:
                        rest_v(1, first + 1)
                rest_u(1, first + AHEAD + 1)
                with dve.Fori(1, AHEAD // 2) as i:
                    for b in range(2):
                        c = first + 2 * i + b
                        dve.wait_ge(ex.summed, c - 1)
                        weigh(b, c, 2 * i + b, acts_ahead[:, bass.ds(2 * i + b, 1), :].rearrange("p o t -> p (o t)"))
                        rest_v(b, c)
                dve.wait_ge(ex.summed, first + AHEAD - 1)
                weigh(0, first + AHEAD, AHEAD, gelu_act[:, 0, :])
                rest_v(0, first + AHEAD)
                rest_u(0, first + AHEAD + 2)
                rest_v(1, first + AHEAD + 1)
                with dve.Fori(AHEAD // 2, NKEYS // 2 - 2) as i:
                    for b, k in ((1, 1), (0, 2)):
                        c = first + 2 * i + k
                        weigh(b, c, 2 * i + k, gelu_act[:, b, :])
                        rest_u(b, c + 2)
                        rest_v(1 - b, c + 1)
                c = first + NKEYS - 3
                weigh(1, c, NKEYS - 3, gelu_act[:, 1, :])
                rest_u(1, c + 2)
                rest_v(0, c + 1)
                weigh(0, c + 1, NKEYS - 2, gelu_act[:, 0, :])
                rest_v(1, c + 2)
                weigh(1, c + 2, NKEYS - 1, gelu_act[:, 1, :])

            dve.wait_ge(s_fgain, 16)
            for tt in range(TT):
                norm_root(LAST, tt)
                dve.scalar_tensor_tensor(h[:, tt, :], summed(tt), rstd[:, tt:tt + 1], expert_v[:, 0, :],
                                         ALU.mult, ALU.mult).then_inc(s_y, 1)

        @block.gpsimd
        def _(pool):
            for n in range(LAYERS):
                s = L[n]
                with pool.Fori(0, UNITS // 2) as i:
                    for b in range(2):
                        pool.wait_ge(ex.unit_hi, n * UNITS + 2 * i + b + 1)
                        for part in range(2):
                            last = pool.tensor_tensor(unit_lo[b][:, part], w_unit[:, b, :, part * P:(part + 1) * P],
                                                      unit_hi[b][:, part].bitcast(F32), ALU.subtract)
                        last.then_inc(ex.unit_split, 1)
                with pool.Fori(0, HEADS) as i:
                    for b in range(2):
                        pool.wait_ge(ex.wq_hi, n * HALVES + 2 * i + b + 1)
                        pool.tensor_tensor(u_lo[:, b], expert_u[:, b], u_hi[:, b].bitcast(F32),
                                           ALU.subtract).then_inc(ex.wq_split, 1)
                def rest_u(b, c, src):
                    pool.wait_ge(ex.u_hi, c + 1)
                    pool.tensor_tensor(u_lo[:, b], src, u_hi[:, b].bitcast(F32), ALU.subtract).then_inc(ex.u_split, 1)

                for b in range(2):
                    rest_u(b, n * NKEYS + b, first_u(b))
                with pool.Fori(1, AHEAD // 2) as i:
                    for b in range(2):
                        rest_u(b, n * NKEYS + 2 * i + b, expert_u[:, b])

                pool.wait_ge(s.picksT, 2)
                with pool.Fori(0, SEQ // TOK_BODY) as i:
                    for g in range(HOT_SLOTS):
                        pool.wait_ge(s.hot, HOT_SLOTS * i + g + 1)
                        t = TOK_BODY * i + TOK_GROUP * g
                        pool.tensor_tensor(onehots[g][:, 0, :, :], onehots[g][:, 0, :, :],
                                           picksT[:, 2, bass.ds(t, TOK_GROUP)].unsqueeze(2)
                                           .to_broadcast([P, TOK_GROUP, P]), ALU.mult).then_inc(s.gated, 1)


def _t5_bucket(dist):
    exact = BUCKETS // 2
    d = np.maximum(dist, 1).astype(np.float32)
    large = exact + (np.log(d / np.float32(exact)).astype(np.float32) / np.float32(math.log(MAX_DISTANCE / exact))
                     * np.float32(BUCKETS - exact)).astype(np.int32)
    return np.where(dist < exact, dist, np.minimum(large, BUCKETS - 1))


def _constants():
    dist = SEQ - 1 - np.arange(SPAN)
    bucket = _t5_bucket(np.maximum(dist, 0))
    onehot = (np.arange(BUCKETS)[:, None] == bucket[None, :]).astype(np.float32)
    mult = sum(((dist % d == 0) & (dist <= w)).astype(np.float64) for w, d in BRANCHES)
    row_a = np.where((dist >= 0) & (mult > 0), np.log(np.maximum(mult, 1)), MASKED)
    row_b = np.where(dist >= 0, 0.0, MASKED)
    rowmask = np.stack([row_a] * A_HEADS + [row_b] * B_HEADS).astype(np.float32)
    p, k = np.arange(P)[:, None], np.arange(SEQ)[None, :]
    mask8 = np.where(P + p - k >= 0, 0.0, MASKED / SCALE).astype(np.float32)
    tri = np.stack([(p + P * t <= k) for t in range(TT)], 1).astype(np.float32)
    iota = np.broadcast_to(np.arange(P, dtype=np.float32), (P, P)).copy()
    return {"c_bucket": onehot, "c_rowmask": rowmask, "c_mask8": mask8, "c_tri": tri, "c_iota": iota,
            "c_ident": np.eye(P, dtype=np.float32), "c_flip": np.eye(P, dtype=np.float32)[::-1]}


def _layout(v):
    def rows(w):
        return np.swapaxes(w.reshape(w.shape[:-2] + (KT, P, w.shape[-1])), -3, -2)

    def units(w, starts, parts):
        return np.stack([np.concatenate([rows(w)[:, :, c:c + P] for c in cols[:parts]], -1) for cols in starts])

    ev, od = v["even_w_in"][0], v["odd_w_in"][0]
    wa = A_HEADS * HEAD
    even = [(3 * wa + P * u, 3 * wa + wa + P * u, 3 * wa + 2 * wa + P * u) for u in range(4)] + \
           [(P * u, wa + P * u, 2 * wa + P * u) for u in range(4)]
    even_out = np.concatenate([v["even_w_out"][0][wa:], v["even_w_out"][0][:wa]])
    odd = [(P * u, D + P * u, 2 * D + P * u) for u in range(UNITS)]
    wq = v["peer_wq"]
    u = v["peer_u"].reshape(LAYERS, NKEYS, NKEYS, KT, P)
    return {
        "x": v["x"],
        "mix_g": np.swapaxes(v["norm_mix_g"].reshape(LAYERS, KT, P), 1, 2),
        "ffn_g": np.swapaxes(v["norm_ffn_g"].reshape(LAYERS, KT, P), 1, 2),
        "final_g": v["final_norm_g"],
        "rel_bias": v["rel_bias"],
        "diff_lambda": v["diff_lambda"].reshape(-1),
        "diff_ln_g": v["diff_ln_g"].reshape(-1),
        "odd_b_f": v["odd_b_f"].reshape(-1),
        "w_f": rows(od)[:, :, 3 * D:],
        "w_qk": np.stack([units(ev, even, 2), units(od, odd, 2)]),
        "w_value": np.stack([units(ev, [c[2:] for c in even], 1), units(od, [c[2:] for c in odd], 1)]),
        "w_out": np.stack([rows(even_out), rows(v["odd_w_out"][0])]),
        "w_query": np.transpose(wq.reshape(LAYERS, KT, P, HALVES, P), (0, 3, 2, 1, 4)),
        "subkeys": np.transpose(v["peer_subkeys"].reshape(LAYERS, HALVES, NKEYS, P), (0, 3, 1, 2)),
        "peer_u": np.transpose(u, (0, 2, 4, 3, 1)),
        "peer_v": v["peer_v"].reshape(LAYERS, NKEYS, NKEYS, D),
    }


def kernel(**inputs):
    import concourse.bacc as bacc
    from concourse.bass_utils import run_bass_kernel_spmd

    data = _layout({k: np.asarray(v) for k, v in inputs.items()})
    data.update(_constants())
    nc = bacc.Bacc("TRN2", target_bir_lowering=False, num_devices=1, dynamic_dma_scratch_size=8192)
    arrays, aps = {}, {}
    for name, arr in data.items():
        arrays["in_" + name] = np.ascontiguousarray(arr)
        aps[name] = nc.dram_tensor("in_" + name, arr.shape, F32, kind="ExternalInput").ap()
    aps["y"] = nc.dram_tensor("out_y", (1, SEQ, D), F32, kind="ExternalOutput").ap()
    build(nc, aps)
    r = run_bass_kernel_spmd(nc, [arrays], core_ids=[0])
    return r.results[0]["out_y"]
```
